# Optimizing a Trainium2 kernel written in Bass

```python
import math
import jax, jax.numpy as jnp
from jax import lax
import numpy as np

D_MODEL = 1024
BATCH = 1
SEQ = 512
DEPTH = 2

D_MIX = D_MODEL
D_CONV = D_MIX // 2
CONV_WIDTH = 31
CONV_PAD = CONV_WIDTH // 2
HEAD_DIM = 64
N_Q_HEADS = (D_MIX - D_CONV) // HEAD_DIM
N_KV_HEADS = 2
GQA_GROUP = N_Q_HEADS // N_KV_HEADS
D_ATTN = N_Q_HEADS * HEAD_DIM
D_KV = N_KV_HEADS * HEAD_DIM
D_IN = 2 * D_CONV + D_ATTN + 2 * D_KV
WINDOW = 128
BLOCK = 128
D_FF = 2816
EPS = 1e-6

kernel_name = "hybrid_conformer_conv_swa_alibi_macaron"

def alibi_slopes(n_heads):
    return np.asarray([2.0 ** (-8.0 * (h + 1) / n_heads) for h in range(n_heads)], dtype=np.float32)

def rmsnorm(x, g):
    xf = x.astype(jnp.float32)
    y = xf * lax.rsqrt(jnp.mean(xf * xf, axis=-1, keepdims=True) + EPS)
    return (y * g.astype(jnp.float32)).astype(x.dtype)

def layernorm(x, g, b):
    xf = x.astype(jnp.float32)
    mu = jnp.mean(xf, axis=-1, keepdims=True)
    var = jnp.mean(jnp.square(xf - mu), axis=-1, keepdims=True)
    y = (xf - mu) * lax.rsqrt(var + EPS)
    return (y * g.astype(jnp.float32) + b.astype(jnp.float32)).astype(x.dtype)

def swiglu(x, w_gate, w_up, w_down):
    return (jax.nn.silu(x @ w_gate) * (x @ w_up)) @ w_down

def conformer_conv(u, conv_w, conv_b, ln_g, ln_b):
    a, gate = jnp.split(u, 2, axis=-1)
    h = a * jax.nn.sigmoid(gate)
    h = lax.conv_general_dilated(
        h, conv_w[:, None, :].astype(h.dtype),
        window_strides=(1,), padding=[(CONV_PAD, CONV_PAD)],
        dimension_numbers=("NWC", "WIO", "NWC"),
        feature_group_count=D_CONV) + conv_b
    h = layernorm(h, ln_g, ln_b)
    return jax.nn.silu(h)

def windowed_gqa_sink(q, k, v, sink):
    B, S, _ = q.shape
    nb = S // BLOCK
    q = q.reshape(B, nb, BLOCK, N_KV_HEADS, GQA_GROUP, HEAD_DIM)
    pad = ((0, 0), (WINDOW, WINDOW), (0, 0))
    kp = jnp.pad(k, pad).reshape(B, nb + 2, BLOCK, N_KV_HEADS, HEAD_DIM)
    vp = jnp.pad(v, pad).reshape(B, nb + 2, BLOCK, N_KV_HEADS, HEAD_DIM)
    kb = jnp.concatenate([kp[:, 0:nb], kp[:, 1:nb + 1], kp[:, 2:nb + 2]], axis=2)
    vb = jnp.concatenate([vp[:, 0:nb], vp[:, 1:nb + 1], vp[:, 2:nb + 2]], axis=2)

    scale = 1.0 / math.sqrt(HEAD_DIM)
    scores = jnp.einsum("bnqkgd,bnskd->bnkgqs", q, kb).astype(jnp.float32) * scale

    dist = (jnp.arange(BLOCK)[:, None] + BLOCK) - jnp.arange(3 * BLOCK)[None, :]
    key_pos = jnp.arange(nb)[:, None] * BLOCK - BLOCK + jnp.arange(3 * BLOCK)[None, :]
    valid = (jnp.abs(dist) <= WINDOW)[None] & ((key_pos >= 0) & (key_pos < S))[:, None, :]

    slopes = jnp.asarray(alibi_slopes(N_Q_HEADS)).reshape(N_KV_HEADS, GQA_GROUP)
    bias = -slopes[:, :, None, None] * jnp.abs(dist).astype(jnp.float32)
    scores = jnp.where(valid[None, :, None, None], scores + bias[None, None], -jnp.inf)

    sink_b = sink.astype(jnp.float32).reshape(N_KV_HEADS, GQA_GROUP)[None, None, :, :, None, None]
    m = jnp.maximum(jnp.max(scores, axis=-1, keepdims=True), sink_b)
    p = jnp.exp(scores - m)
    denom = jnp.sum(p, axis=-1, keepdims=True) + jnp.exp(sink_b - m)
    o = jnp.einsum("bnkgqs,bnskd->bnqkgd", (p / denom).astype(v.dtype), vb)
    return o.reshape(B, S, D_ATTN)

def setup_inputs(seed: int = 0) -> dict:
    key = jax.random.key(seed)
    ks = jax.random.split(key, 24)
    f32 = jnp.float32

    def nrm(k, shape, scale):
        return jax.random.normal(k, shape, f32) * scale

    def gain(k, shape):
        return 1.0 + 0.02 * jax.random.normal(k, shape, f32)

    return {
        "x": jax.random.normal(ks[0], (BATCH, SEQ, D_MODEL), f32),
        "ffn1_norm": gain(ks[1], (DEPTH, D_MODEL)),
        "ffn1_w_gate": nrm(ks[2], (DEPTH, D_MODEL, D_FF), D_MODEL ** -0.5),
        "ffn1_w_up": nrm(ks[3], (DEPTH, D_MODEL, D_FF), D_MODEL ** -0.5),
        "ffn1_w_down": nrm(ks[4], (DEPTH, D_FF, D_MODEL), D_FF ** -0.5),
        "mix_norm": gain(ks[5], (DEPTH, D_MODEL)),
        "w_in": nrm(ks[6], (DEPTH, D_MODEL, D_IN), D_MODEL ** -0.5),
        "conv_w": nrm(ks[7], (DEPTH, CONV_WIDTH, D_CONV), CONV_WIDTH ** -0.5),
        "conv_b": nrm(ks[8], (DEPTH, D_CONV), 0.01),
        "conv_ln_g": gain(ks[9], (DEPTH, D_CONV)),
        "conv_ln_b": nrm(ks[10], (DEPTH, D_CONV), 0.01),
        "attn_sink": nrm(ks[11], (DEPTH, N_Q_HEADS), 0.5),
        "out_norm_conv": gain(ks[12], (DEPTH, D_CONV)),
        "out_norm_attn": gain(ks[13], (DEPTH, D_ATTN)),
        "w_out": nrm(ks[14], (DEPTH, D_MIX, D_MODEL), D_MIX ** -0.5),
        "ffn2_norm": gain(ks[15], (DEPTH, D_MODEL)),
        "ffn2_w_gate": nrm(ks[16], (DEPTH, D_MODEL, D_FF), D_MODEL ** -0.5),
        "ffn2_w_up": nrm(ks[17], (DEPTH, D_MODEL, D_FF), D_MODEL ** -0.5),
        "ffn2_w_down": nrm(ks[18], (DEPTH, D_FF, D_MODEL), D_FF ** -0.5),
        "final_norm": gain(ks[19], (D_MODEL,)),
    }

def reference(x, ffn1_norm, ffn1_w_gate, ffn1_w_up, ffn1_w_down, mix_norm, w_in,
              conv_w, conv_b, conv_ln_g, conv_ln_b, attn_sink, out_norm_conv,
              out_norm_attn, w_out, ffn2_norm, ffn2_w_gate, ffn2_w_up, ffn2_w_down,
              final_norm):
    c0 = 2 * D_CONV
    c1 = c0 + D_ATTN
    c2 = c1 + D_KV
    for l in range(DEPTH):
        x = x + 0.5 * swiglu(rmsnorm(x, ffn1_norm[l]), ffn1_w_gate[l], ffn1_w_up[l], ffn1_w_down[l])
        h = rmsnorm(x, mix_norm[l])
        u = h @ w_in[l]
        y_conv = conformer_conv(u[..., :c0], conv_w[l], conv_b[l], conv_ln_g[l], conv_ln_b[l])
        y_attn = windowed_gqa_sink(u[..., c0:c1], u[..., c1:c2], u[..., c2:], attn_sink[l])
        y = jnp.concatenate([rmsnorm(y_conv, out_norm_conv[l]),
                             rmsnorm(y_attn, out_norm_attn[l])], axis=-1)
        x = x + y @ w_out[l]
        x = x + 0.5 * swiglu(rmsnorm(x, ffn2_norm[l]), ffn2_w_gate[l], ffn2_w_up[l], ffn2_w_down[l])
    return rmsnorm(x, final_norm)


_drawn_inputs = setup_inputs


def setup_inputs(seed=0):
    import zlib

    import numpy as np

    out = dict(_drawn_inputs(seed))
    spreads = {}
    factors = {'ffn1_norm': 4.496,
     'conv_b': 3.895,
     'conv_ln_g': 12.707,
     'conv_ln_b': 27.69,
     'out_norm_conv': 18.704,
     'out_norm_attn': 16.702,
     'ffn2_norm': 7.03,
     'final_norm': 8.002}
    for name, (base, spread) in spreads.items():
        noise = np.random.default_rng([zlib.crc32(name.encode()), seed]).standard_normal(out[name].shape)
        drawn = base * np.exp(spread * noise) if base else spread * noise
        out[name] = __import__('jax').numpy.asarray(drawn.astype(out[name].dtype))
    for name, factor in factors.items():
        out[name] = (out[name] * factor).astype(out[name].dtype)
    return out
```

```python
import math
from contextlib import ExitStack

import numpy as np

import concourse.bass as bass
from concourse import mybir

P = 128
D_MODEL, SEQ, DEPTH, D_FF = 1024, 512, 2, 2816
D_CONV, CONV_WIDTH, HEAD_DIM = 512, 31, 64
N_Q_HEADS, N_KV_HEADS = 8, 2
GROUP = N_Q_HEADS // N_KV_HEADS
CONV_PAD = CONV_WIDTH // 2
EPS = 1e-6
MASKED = 1e30

ND = D_MODEL // P
NF = D_FF // P
NC = D_CONV // P
NB = SEQ // P
RING = 4
BANKS = 4
DOWN = (6, 6, 5, 5)
assert sum(DOWN) == NF

IN_TILES = ["a0", "g0", "a1", "g1", "k", "v", "q0", "q1", "q2", "q3", "a2", "g2", "a3", "g3"]
IN_SLOTS = [(t,) for t in range(12)] + [(12, 0), (12, 1), (13, 0), (13, 1)]

FFN_SLOTS, MIX_SLOTS = 2 * NF + 4 * ND, 24
LAYER_SLOTS = 2 * FFN_SLOTS + MIX_SLOTS
FFN_TURNS, MIX_TURNS = 2 * NF + ND, 32
LAYER_TURNS = 2 * FFN_TURNS + MIX_TURNS
OUT_A_TURN, OUT_C_TURN = 16, 24
assert LAYER_SLOTS % RING == 0 and LAYER_TURNS % BANKS == 0

STATS = ["ffn1", "mix", "attn", "mean", "var", "conv", "ffn2"]
ROOTS = [s for s in STATS if s != "mean"]

G_MIX, G_FFN2, G_NEXT = 0, 8, 16
CONV_W = 24
CONV_B = CONV_W + NC * CONV_WIDTH
LN_G, LN_B, G_CONV, G_ATTN = CONV_B + 4, CONV_B + 8, CONV_B + 12, CONV_B + 16
SINK = CONV_B + 20
N_PAR = SINK + N_Q_HEADS

ALU = mybir.AluOpType
ACT = mybir.ActivationFunctionType
F32 = mybir.dt.float32
F32R = mybir.dt.float32r
I32 = mybir.dt.int32


def keys_of(b):
    first = max(0, b - 1)
    return first, min(NB, b + 2) - first


def slope(kv, c):
    return 2.0 ** (-8.0 * (kv * GROUP + c + 1) / N_Q_HEADS)


def attention_turns():
    turns = [("scores", 0, c) for c in range(GROUP)]
    for g in range(2 * NB):
        for c in range(GROUP):
            if g + 1 < 2 * NB:
                turns.append(("scores", g + 1, c))
            turns.append(("turned", g, c))
    return {use: n for n, use in enumerate(turns)}


ATT = attention_turns()
ATT_BANKS = 3
N_GROUPS = 2 * NB
N_UNITS = N_GROUPS * GROUP
TAP_OPS = CONV_WIDTH + 1


def encoder(nc, xT, first_gain, params, w_gu, w_down, w_in, w_out, out):
    with ExitStack() as ctx:
        def sb(name, shape, dt=F32, stack=ctx):
            return stack.enter_context(nc.sbuf_tensor(name, shape, dt))

        def sem(name):
            return ctx.enter_context(nc.semaphore(name))

        x = sb("x", [P, ND, SEQ])
        xs_hi = sb("xs_hi", [P, ND, SEQ], F32R)
        xs_lo = sb("xs_lo", [P, ND, SEQ], F32R)
        stage = sb("stage", [P, RING, 8 * P])
        w_hi = sb("w_hi", [P, RING, 8 * P], F32R)
        w_lo = sb("w_lo", [P, RING, 8 * P], F32R)
        work = sb("work", [P, BANKS, SEQ])
        sq = sb("sq", [P, SEQ])
        sq_sum = sb("sq_sum", [P, SEQ])
        zeros = sb("zeros", [P, SEQ])
        std = sb("std", [P, SEQ])
        rstd = sb("rstd", [P, SEQ])
        dist = sb("dist", [P, 3 * P])
        ident = sb("ident", [P, P])
        ones = sb("ones", [P, P])
        q_scale = sb("q_scale", [P, NC])
        eps = sb("eps", [P, 1])
        gain0 = sb("gain0", [P, ND])
        par = sb("par", [P, N_PAR])
        neg_sink = sb("neg_sink", [P, N_Q_HEADS])
        neg_max = sb("neg_max", [P, 2, GROUP])
        p_sum = sb("p_sum", [P, 2, GROUP])
        sink_arg = sb("sink_arg", [P, 2, GROUP])
        sink_exp = sb("sink_exp", [P, 2, GROUP])
        den = sb("den", [P, 2, GROUP])
        r_den = sb("r_den", [P, 2, GROUP])

        with ExitStack() as region:
            h_hi = sb("h_hi", [P, NF, SEQ], F32R, region)
            h_lo = sb("h_lo", [P, NF, SEQ], F32R, region)
        with ExitStack() as region:
            prob = sb("prob", [P, 2, GROUP, 3 * P], F32, region)
            pt_hi = sb("pt_hi", [P, 2, 3, GROUP, P], F32R, region)
            pt_lo = sb("pt_lo", [P, 2, 3, GROUP, P], F32R, region)
            glu = sb("glu", [P, NC, SEQ + 2 * CONV_PAD], F32, region)
            y_conv = sb("y_conv", [P, NC, SEQ], F32, region)
            odd_taps = sb("odd_taps", [P, SEQ], F32, region)
            q_hi = sb("q_hi", [P, NC, SEQ], F32R, region)
            q_lo = sb("q_lo", [P, NC, SEQ], F32R, region)
            k_hi = sb("k_hi", [P, SEQ], F32R, region)
            k_lo = sb("k_lo", [P, SEQ], F32R, region)
            v_hi = sb("v_hi", [P, NB, P], F32R, region)
            v_lo = sb("v_lo", [P, NB, P], F32R, region)
            y_attn = sb("y_attn", [P, NC, SEQ], F32, region)
        y_hi, y_lo = q_hi, q_lo
        with ExitStack() as region:
            result = sb("result", [P, ND, SEQ], F32, region)
            dist_int = sb("dist_int", [P, 3 * P], I32, region)
            dist_neg = sb("dist_neg", [P, 3 * P], F32, region)

        bank = [ctx.enter_context(nc.psum_tensor(f"bank{i}", [P, SEQ], F32)) for i in range(8)]
        att_bank, side_bank = bank[4:7], bank[7]

        landed = [sem(f"landed{i}") for i in range(RING)]
        in_landed = sem("in_landed")
        par_landed = sem("par_landed")
        hi_made = sem("hi_made")
        split = sem("split")
        used = sem("used")
        half_used = sem("half_used")
        evicted = sem("evicted")
        silu_made = sem("silu_made")
        h_made = sem("h_made")
        h_hi_made = sem("h_hi_made")
        h_split = sem("h_split")
        x_made = sem("x_made")
        x_half = sem("x_half")
        x_hi_made = sem("x_hi_made")
        x_split = sem("x_split")
        squared = sem("squared")
        sq_added = sem("sq_added")
        stat_made = sem("stat_made")
        std_made = sem("std_made")
        rstd_made = sem("rstd_made")
        consts_v = sem("consts_v")
        consts_p = sem("consts_p")
        small_made = sem("small_made")
        padded = sem("padded")
        sig_made = sem("sig_made")
        glu_made = sem("glu_made")
        tapped = sem("tapped")
        qk_hi = sem("qk_hi")
        qk_split = sem("qk_split")
        v_turned = sem("v_turned")
        v_hi_made = sem("v_hi_made")
        v_split = sem("v_split")
        scored = sem("scored")
        att_freed = sem("att_freed")
        exped = sem("exped")
        sink_ready = sem("sink_ready")
        sink_exped = sem("sink_exped")
        den_made = sem("den_made")
        r_den_made = sem("r_den_made")
        normed = sem("normed")
        turned = sem("turned")
        pt_hi_made = sem("pt_hi_made")
        o_made = sem("o_made")
        o_evicted = sem("o_evicted")
        y_hi_made = sem("y_hi_made")
        y_split = sem("y_split")
        y_squared = sem("y_squared")
        centred = sem("centred")
        ln_scaled = sem("ln_scaled")
        ln_silu = sem("ln_silu")
        neg_sink_made = sem("neg_sink_made")
        result_made = sem("result_made")
        stored = sem("stored")

        def slot_no(l, n):
            return l * LAYER_SLOTS + n

        def turn_no(l, n):
            return l * LAYER_TURNS + n

        def stat_no(l, name):
            return l * len(STATS) + STATS.index(name)

        def root_no(l, name):
            return l * len(ROOTS) + ROOTS.index(name)

        def prep_no(l, which):
            return l * 3 + which

        def chunk(t, m):
            return t[:, m, :] if isinstance(m, int) else t[:, bass.ds(m, 1), :].rearrange("p o n -> p (o n)")

        def column(t, m):
            return t[:, m:m + 1] if isinstance(m, int) else t[:, bass.ds(m, 1)]

        FFNS = [(0, 0, 0, 0, "ffn1"), (FFN_SLOTS + MIX_SLOTS, FFN_TURNS + MIX_TURNS, NF, 2, "ffn2")]
        MIX_S, MIX_T = FFN_SLOTS, FFN_TURNS
        TAPS_PER_TILE, TAPS_PER_GROUP = 5, 8

        block = ctx.enter_context(nc.Block())

        @block.sync
        def _(sp):
            sp.dma_start(gain0[:], first_gain).then_inc(in_landed, 16)
            sp.dma_start(x[:], xT.rearrange("(k p) n -> p k n", p=P)).then_inc(in_landed, 16)

            def load(l, n, r, src, width):
                sp.wait_ge(split, slot_no(l, n) + 1)
                sp.dma_start(stage[:, r, 0:width], src).then_inc(landed[r], 16)

            def ffn_loads(l, which, base):
                with sp.Fori(0, 2 * NF // RING) as i:
                    for j in range(RING):
                        src = w_gu[bass.ds(l, 1), which, bass.ds(i * RING + j, 1)]
                        load(l, base + i * RING + j, j, src.rearrange("o t p n -> p (o t n)"), 8 * P)
                if which == 0:
                    sp.wait_ge(x_split, prep_no(l, 0) * ND + ND)
                    sp.dma_start(par[:], params[bass.ds(l, 1)].rearrange("o p n -> p (o n)")).then_inc(par_landed, 16)
                with sp.Fori(0, ND) as m:
                    at = 0
                    for j, count in enumerate(DOWN):
                        src = w_down[bass.ds(l, 1), which, bass.ds(m, 1), :, at:at + count * P]
                        load(l, base + 2 * NF + m * 4 + j, j, src.rearrange("o t p n -> p (o t n)"), count * P)
                        at += count * P

            with sp.Fori(0, DEPTH) as l:
                ffn_loads(l, 0, 0)
                for s, (t, *half) in enumerate(IN_SLOTS):
                    width = 4 * P if half else 8 * P
                    start = 4 * P * half[0] if half else 0
                    src = w_in[bass.ds(l, 1), t, :, start:start + width].rearrange("o p n -> p (o n)")
                    load(l, MIX_S + s, s % RING, src, width)
                for s in range(8):
                    src = w_out[bass.ds(l, 1), s].rearrange("o p n -> p (o n)")
                    load(l, MIX_S + 16 + s, s % RING, src, 8 * P)
                ffn_loads(l, 1, FFN_SLOTS + MIX_SLOTS)

            out_v = out.rearrange("(k p) n -> p k n", p=P)
            for m in range(ND):
                sp.wait_ge(result_made, m + 1)
                sp.dma_start(out_v[:, m, :], result[:, m, :]).then_inc(stored, 16)
            sp.wait_ge(stored, 16 * ND)

        @block.gpsimd
        def _(pool):
            pool.sem_inc(split, RING)
            nc.gpsimd.iota(dist_int[:], pattern=[[-1, 3 * P]], base=P, channel_multiplier=1).then_inc(consts_p, 1)
            nc.gpsimd.memset(ident[:], 0.0).then_inc(consts_p, 1)
            pool.wait_ge(consts_p, 2)
            nc.gpsimd.affine_select(out=ident[:], in_=ident[:], compare_op=ALU.not_equal, fill=1.0, base=0,
                                    pattern=[[-1, P]], channel_multiplier=1).then_inc(consts_p, 1)
            pool.wait_ge(consts_v, 3)
            nc.gpsimd.affine_select(out=dist[:], in_=dist[:], compare_op=ALU.is_ge, fill=MASKED, base=0,
                                    pattern=[[1, 3 * P]], channel_multiplier=-1).then_inc(consts_p, 1)
            pool.wait_ge(consts_p, 4)
            nc.gpsimd.affine_select(out=dist[:], in_=dist[:], compare_op=ALU.is_ge, fill=MASKED, base=2 * P,
                                    pattern=[[-1, 3 * P]], channel_multiplier=1).then_inc(consts_p, 1)

            def low(l, n, r):
                pool.wait_ge(hi_made, slot_no(l, n) + 1)
                nc.gpsimd.tensor_tensor(w_lo[:, r, :], stage[:, r, :], w_hi[:, r, :].bitcast(F32),
                                        ALU.subtract).then_inc(split, 1)

            def add_square(prep, m, first=False):
                pool.wait_ge(squared, prep * ND + m + 1)
                if not first:
                    pool.wait_ge(sq_added, prep * ND + m)
                nc.gpsimd.tensor_tensor(sq_sum[:], zeros[:] if first else sq_sum[:], sq[:],
                                        ALU.add).then_inc(sq_added, 1)

            def ffn_steps(l, base, next_prep, last):
                with pool.Fori(0, NF // 2) as i:
                    for j in range(4):
                        low(l, base + i * 4 + j + RING, j)
                at = base + 2 * NF
                for j in range(4):
                    low(l, at + RING + j, j)
                add_square(next_prep, 0, first=True)
                with pool.Fori(1, ND - 1) as m:
                    for j in range(4):
                        low(l, at + m * 4 + RING + j, j)
                    add_square(next_prep, m)
                if not last:
                    for j in range(4):
                        low(l, at + ND * 4 + j, j)
                add_square(next_prep, ND - 1)

            pool.wait_ge(small_made, 1)
            for m in range(ND):
                add_square(0, m, first=m == 0)
            with pool.Fori(0, DEPTH) as l:
                for j in range(RING):
                    low(l, j, j)
                ffn_steps(l, 0, prep_no(l, 1), last=False)
                for s in range(16):
                    low(l, MIX_S + s + RING, s % RING)
                for s in range(4):
                    low(l, MIX_S + 16 + s + RING, s % RING)
                    for m in (2 * s, 2 * s + 1):
                        pool.wait_ge(evicted, turn_no(l, MIX_T + OUT_A_TURN + m) + 1 + BANKS)
                        nc.gpsimd.tensor_tensor(x[:, m, :], x[:, m, :], work[:, m % BANKS, :],
                                                ALU.add).then_inc(x_half, 1)
                for s in range(4):
                    low(l, MIX_S + 20 + s + RING, s % RING)
                    for m in (2 * s, 2 * s + 1):
                        add_square(prep_no(l, 2), m, first=m == 0)
                ffn_steps(l, FFN_SLOTS + MIX_SLOTS, prep_no(l, 3), last=True)

        @block.scalar
        def _(act):
            def high(l, n, r, uses):
                act.wait_ge(landed[r], uses * 16 + 16)
                act.wait_ge(used, slot_no(l, n) + 1)
                nc.scalar.activation(w_hi[:, r, :], stage[:, r, :], ACT.Copy).then_inc(hi_made, 1)

            def uses_of(l, n, r):
                return l * (LAYER_SLOTS // RING) + n

            def prepare(prep, m, gain, gain_at, first=False):
                nc.scalar.activation(xs_hi[:, m, :], x[:, m, :], ACT.Copy,
                                     scale=gain[:, gain_at + m:gain_at + m + 1]).then_inc(x_hi_made, 1)
                if not (first and m == 0):
                    act.wait_ge(sq_added, prep * ND + m)
                nc.scalar.activation(sq[:], x[:, m, :], ACT.Square).then_inc(squared, 1)

            def root(l, name, source, count):
                act.wait_ge(stat_made, stat_no(l, name) + 1)
                act.wait_ge(rstd_made, root_no(l, name) + 1)
                nc.scalar.activation(std[:], source[:], ACT.Sqrt, bias=eps[:], scale=1.0 / count).then_inc(std_made, 1)

            def ffn_steps(l, base, turns, name, last):
                root(l, name, side_bank, D_MODEL)
                with act.Fori(0, NF // 2) as i:
                    for j in range(2):
                        f = i * 2 + j
                        high(l, base + f * 2 + RING, 2 * j, uses_of(l, base // RING + 1 + i, 0))
                        act.wait_ge(evicted, turn_no(l, turns + f * 2) + 1 + BANKS)
                        nc.scalar.activation(work[:, 2 * j, :], work[:, 2 * j, :], ACT.Silu).then_inc(silu_made, 1)
                        high(l, base + f * 2 + 1 + RING, 2 * j + 1, uses_of(l, base // RING + 1 + i, 0))
                at = base + 2 * NF

                def down(m):
                    for j in range(4):
                        high(l, at + m * 4 + RING + j, j, uses_of(l, at // RING + 1 + m, 0))

                with act.Fori(0, ND - 1) as m:
                    down(m)
                if not last:
                    down(ND - 1)

            act.wait_ge(small_made, 1)
            act.wait_ge(in_landed, 32)
            for m in range(ND):
                prepare(0, m, gain0, 0, first=True)
            with act.Fori(0, DEPTH) as l:
                for j in range(RING):
                    high(l, j, j, uses_of(l, 0, 0))
                ffn_steps(l, 0, 0, "ffn1", last=False)

                def mix_high(s):
                    high(l, MIX_S + s + RING, s % RING, uses_of(l, (MIX_S + s) // RING + 1, 0))

                def tile_ready(t):
                    act.wait_ge(evicted, turn_no(l, MIX_T + t) + 1 + BANKS)

                def sigmoid(c, t):
                    tile_ready(t)
                    nc.scalar.activation(work[:, t % BANKS, :], work[:, t % BANKS, :],
                                         ACT.Sigmoid).then_inc(sig_made, 1)

                def exp_scores(g, c):
                    b, kv = divmod(g, 2)
                    n = keys_of(b)[1] * P
                    unit = prob[:, g % 2, c, 0:n]
                    act.wait_ge(att_freed, l * len(ATT) + ATT["scores", g, c] + 1)
                    nc.scalar.activation(unit, unit, ACT.Exp, bias=neg_max[:, g % 2, c:c + 1], scale=-1.0,
                                         accum_out=p_sum[:, g % 2, c:c + 1]).then_inc(exped, 1)

                def exp_sink(g):
                    act.wait_ge(sink_ready, l * N_GROUPS + g + 1)
                    nc.scalar.activation(sink_exp[:, g % 2, :], sink_arg[:, g % 2, :], ACT.Exp).then_inc(sink_exped, 1)

                def normalise(g):
                    act.wait_ge(r_den_made, l * N_GROUPS + g + 1)
                    act.wait_ge(exped, l * N_UNITS + g * GROUP + GROUP)
                    for c in range(GROUP):
                        unit = prob[:, g % 2, c, 0:keys_of(g // 2)[1] * P]
                        nc.scalar.activation(unit, unit, ACT.Copy, scale=r_den[:, g % 2, c:c + 1]).then_inc(normed, 1)

                def turned_high(g, c):
                    n = keys_of(g // 2)[1]
                    act.wait_ge(turned, l * N_UNITS + g * GROUP + c + 1)
                    if g >= 2 and c == 0:
                        act.wait_ge(o_made, l * N_GROUPS + g - 1)
                    src = att_bank[ATT["turned", g, c] % ATT_BANKS][:, 0:n * P].rearrange("p (k q) -> p k q", q=P)
                    nc.scalar.activation(pt_hi[:, g % 2, 0:n, c, :], src, ACT.Copy).then_inc(pt_hi_made, 1)

                root(l, "mix", side_bank, D_MODEL)
                for t in range(10):
                    mix_high(t)
                    name = IN_TILES[t]
                    if name[0] == "g":
                        sigmoid(int(name[1]), t)
                    elif name == "k":
                        tile_ready(t)
                        nc.scalar.activation(k_hi[:], work[:, t % BANKS, :], ACT.Copy).then_inc(qk_hi, 1)
                    elif name[0] == "q":
                        c = int(name[1])
                        tile_ready(t)
                        nc.scalar.activation(q_hi[:, c, :], work[:, t % BANKS, :], ACT.Copy).then_inc(qk_hi, 1)
                        if c == 0:
                            act.wait_ge(v_turned, l + 1)
                            nc.scalar.activation(v_hi[:].rearrange("p b d -> p (b d)"), side_bank[:],
                                                 ACT.Copy).then_inc(v_hi_made, 1)
                for c in range(GROUP):
                    exp_scores(0, c)
                exp_sink(0)
                normalise(0)
                mix_high(10)
                for g in range(N_GROUPS):
                    for c in range(GROUP):
                        if g + 1 < N_GROUPS:
                            exp_scores(g + 1, c)
                        turned_high(g, c)
                    if g + 1 < N_GROUPS:
                        exp_sink(g + 1)
                        normalise(g + 1)
                    if g == 1:
                        mix_high(11)
                        sigmoid(2, 11)
                    elif g == 3:
                        mix_high(12)
                        mix_high(13)
                    elif g == 5:
                        mix_high(14)
                        mix_high(15)
                        sigmoid(3, 13)

                for c in range(NC):
                    if c == 0:
                        act.wait_ge(o_evicted, l * N_GROUPS + N_GROUPS)
                        act.wait_ge(glu_made, l * NC + NC)
                    nc.scalar.activation(xs_hi[:, c, :], y_attn[:, c, :], ACT.Copy,
                                         scale=par[:, G_ATTN + c:G_ATTN + c + 1]).then_inc(y_hi_made, 1)
                    nc.scalar.activation(work[:, c, :], y_attn[:, c, :], ACT.Square).then_inc(y_squared, 1)
                root(l, "attn", side_bank, D_CONV)
                for s in range(16, 20):
                    mix_high(s)

                for c in range(NC):
                    if c == 0:
                        act.wait_ge(x_half, l * ND + ND)
                    act.wait_ge(centred, l * NC + c + 1)
                    nc.scalar.activation(work[:, c, :], y_conv[:, c, :], ACT.Square).then_inc(y_squared, 1)
                root(l, "var", att_bank[2], D_CONV)
                for c in range(NC):
                    act.wait_ge(ln_scaled, l * NC + c + 1)
                    nc.scalar.activation(y_conv[:, c, :], y_conv[:, c, :], ACT.Silu,
                                         bias=par[:, LN_B + c:LN_B + c + 1],
                                         scale=par[:, LN_G + c:LN_G + c + 1]).then_inc(ln_silu, 1)
                    act.wait_ge(ln_silu, l * NC + c + 1)
                    nc.scalar.activation(y_hi[:, c, :], y_conv[:, c, :], ACT.Copy,
                                         scale=par[:, G_CONV + c:G_CONV + c + 1]).then_inc(y_hi_made, 1)
                for c in range(NC):
                    nc.scalar.activation(work[:, c, :], y_conv[:, c, :], ACT.Square).then_inc(y_squared, 1)
                root(l, "conv", side_bank, D_CONV)
                for s in range(20, 24):
                    mix_high(s)
                    for m in (2 * (s - 20), 2 * (s - 20) + 1):
                        act.wait_ge(x_made, l * ND + m + 1)
                        prepare(prep_no(l, 2), m, par, G_FFN2)
                ffn_steps(l, FFN_SLOTS + MIX_SLOTS, FFN_TURNS + MIX_TURNS, "ffn2", last=True)
            root(DEPTH, "ffn1", side_bank, D_MODEL)

        @block.vector
        def _(dve):
            dve.sem_inc(evicted, BANKS)
            dve.sem_inc(rstd_made, 1)
            nc.vector.memset(ones[:], 1.0).then_inc(consts_v, 1)
            dve.wait_ge(consts_p, 1)
            nc.vector.tensor_copy(dist[:], dist_int[:]).then_inc(consts_v, 1)
            dve.wait_ge(consts_v, 2)
            nc.vector.tensor_scalar(dist_neg[:], dist[:], -1.0, None, ALU.mult)
            nc.vector.memset(eps[:], EPS)
            nc.vector.memset(zeros[:], 0.0)
            for c in range(NC):
                for kv in range(N_KV_HEADS):
                    nc.vector.memset(q_scale[HEAD_DIM * kv:HEAD_DIM * (kv + 1), c:c + 1],
                                     -1.0 / (math.sqrt(HEAD_DIM) * slope(kv, c)))
            dve.drain().then_inc(small_made, 1)
            dve.wait_ge(small_made, 1)
            nc.vector.tensor_tensor(dist[:], dist[:], dist_neg[:], ALU.max).then_inc(consts_v, 1)

            def split_x(prep, m, gain, gain_at):
                dve.wait_ge(x_hi_made, prep * ND + m + 1)
                nc.vector.scalar_tensor_tensor(chunk(xs_lo, m), chunk(x, m), column(gain, gain_at + m),
                                               chunk(xs_hi, m).bitcast(F32), ALU.mult,
                                               ALU.subtract).then_inc(x_split, 1)

            def recip(l, name):
                dve.wait_ge(std_made, root_no(l, name) + 1)
                nc.vector.reciprocal(rstd[:], std[:]).then_inc(rstd_made, 1)

            def rstd_ready(l, name):
                dve.wait_ge(rstd_made, root_no(l, name) + 2)

            def tile_summed(l, slot):
                dve.wait_ge(used, slot_no(l, slot) + 1 + RING)

            def scale_tile(b, w, inc=1):
                nc.vector.tensor_tensor(work[:, w, :], bank[b][:], rstd[:], ALU.mult).then_inc(evicted, inc)

            def own(l, turn):
                dve.wait_ge(evicted, turn_no(l, turn) + 1 + BANKS)

            def ffn_steps(l, base, turns, h_base, prep, name, gain_at):
                recip(l, name)
                with dve.Fori(0, NF // 2) as i:
                    rstd_ready(l, name)
                    for j in range(2):
                        f = i * 2 + j
                        h_no = l * 2 * NF + h_base + f
                        for part in (2 * j, 2 * j + 1):
                            tile_summed(l, base + i * 4 + part)
                            scale_tile(part, part)
                        own(l, turns + f * 2 + 1)
                        dve.wait_ge(silu_made, h_no + 1)
                        nc.vector.tensor_tensor(work[:, 2 * j + 1, :], work[:, 2 * j, :], work[:, 2 * j + 1, :],
                                                ALU.mult).then_inc(h_made, 1)
                        dve.wait_ge(h_made, h_no + 1)
                        nc.vector.tensor_scalar(chunk(h_hi, f), work[:, 2 * j + 1, :], 1.0, None,
                                                ALU.mult).then_inc(h_hi_made, 1)
                        dve.wait_ge(h_hi_made, h_no + 1)
                        nc.vector.tensor_tensor(chunk(h_lo, f), work[:, 2 * j + 1, :], chunk(h_hi, f).bitcast(F32),
                                                ALU.subtract).then_inc(h_split, 1)
                with dve.Fori(0, ND // 4) as i:
                    dve.wait_ge(par_landed, l * 16 + 16)
                    for j in range(4):
                        m = i * 4 + j
                        tile_summed(l, base + 2 * NF + m * 4 + 3)
                        nc.vector.scalar_tensor_tensor(chunk(x, m), bank[j][:], 0.5, chunk(x, m), ALU.mult,
                                                       ALU.add).then_inc(evicted, 1)
                        own(l, turns + 2 * NF + m)
                        nc.vector.tensor_scalar(chunk(xs_hi, m), chunk(x, m), column(par, gain_at + m), None,
                                                ALU.mult).then_inc(x_hi_made, 1)
                        split_x(prep, m, par, gain_at)
                        dve.wait_ge(sq_added, prep * ND + m)
                        nc.vector.tensor_tensor(sq[:], chunk(x, m), chunk(x, m), ALU.mult).then_inc(squared, 1)

            dve.wait_ge(in_landed, 32)
            for m in range(ND):
                split_x(0, m, gain0, 0)
            with dve.Fori(0, DEPTH) as l:
                ffn_steps(l, 0, 0, 0, prep_no(l, 1), "ffn1", G_MIX)

                def turn(t):
                    return MIX_T + t

                def in_summed(t):
                    tile_summed(l, MIX_S + (t if t < 12 else 13 + 2 * (t - 12)))

                def tile(t, inc=1):
                    in_summed(t)
                    scale_tile(t % BANKS, t % BANKS, inc)

                def out_summed(slot, m):
                    if m % 2:
                        tile_summed(l, MIX_S + slot + m // 2)
                    else:
                        dve.wait_ge(half_used, l * ND + (slot - 16) + m // 2 + 1)

                def gate(c):
                    ta, tg = IN_TILES.index(f"a{c}"), IN_TILES.index(f"g{c}")
                    own(l, turn(ta))
                    dve.wait_ge(sig_made, l * NC + c + 1)
                    nc.vector.tensor_tensor(glu[:, c, CONV_PAD:CONV_PAD + SEQ], work[:, ta % BANKS, :],
                                            work[:, tg % BANKS, :], ALU.mult).then_inc(glu_made, 1)

                def taps(first, count):
                    for n in range(first, first + count):
                        c, t = divmod(n, TAP_OPS)
                        if t == 0:
                            dve.wait_ge(glu_made, l * NC + c + 1)
                        if t < CONV_WIDTH:
                            h = glu[:, c, t:t + SEQ]
                            w = par[:, CONV_W + c * CONV_WIDTH + t:CONV_W + c * CONV_WIDTH + t + 1]
                        into = y_conv[:, c, :] if t % 2 == 0 else odd_taps[:]
                        if t >= 2 or (c and t == 1):
                            dve.wait_ge(tapped, l * NC * TAP_OPS + n - (t < CONV_WIDTH))
                        if t == CONV_WIDTH:
                            nc.vector.tensor_tensor(y_conv[:, c, :], y_conv[:, c, :], odd_taps[:],
                                                    ALU.add).then_inc(tapped, 1)
                        elif t == 0:
                            nc.vector.tensor_scalar(into, h, w, par[:, CONV_B + c:CONV_B + c + 1], ALU.mult,
                                                    ALU.add).then_inc(tapped, 1)
                        elif t == 1:
                            nc.vector.tensor_scalar(into, h, w, None, ALU.mult).then_inc(tapped, 1)
                        else:
                            nc.vector.scalar_tensor_tensor(into, h, w, into, ALU.mult, ALU.add).then_inc(tapped, 1)

                def low_qk(t, n, hi, lo):
                    own(l, turn(t))
                    dve.wait_ge(qk_hi, l * (NC + 1) + n + 1)
                    nc.vector.tensor_tensor(lo, work[:, t % BANKS, :], hi.bitcast(F32),
                                            ALU.subtract).then_inc(qk_split, 1)

                def bias_scores(g, c, first_tap):
                    b, kv = divmod(g, 2)
                    first, n = keys_of(b)
                    at = (first - (b - 1)) * P
                    k = ATT["scores", g, c]
                    dve.wait_ge(consts_p, 5)
                    dve.wait_ge(scored, l * N_UNITS + g * GROUP + c + 1)
                    if g >= 2:
                        dve.wait_ge(turned, l * N_UNITS + (g - 2) * GROUP + c + 1)
                    taps(first_tap, 2)
                    nc.vector.tensor_tensor_reduce(
                        out=prob[:, g % 2, c, 0:n * P], in0=att_bank[k % ATT_BANKS][:, 0:n * P],
                        in1=dist[:, at:at + n * P], scale=slope(kv, c),
                        scalar=neg_sink[:, kv * GROUP + c:kv * GROUP + c + 1], op0=ALU.add, op1=ALU.min,
                        accum_out=neg_max[:, g % 2, c:c + 1]).then_inc(att_freed, 1)

                def sink_args(g):
                    kv = g % 2
                    dve.wait_ge(att_freed, l * len(ATT) + ATT["scores", g, GROUP - 1] + 1)
                    nc.vector.tensor_tensor(sink_arg[:, g % 2, :], neg_max[:, g % 2, :],
                                            par[:, SINK + kv * GROUP:SINK + (kv + 1) * GROUP],
                                            ALU.add).then_inc(sink_ready, 1)

                def denominators(g):
                    dve.wait_ge(sink_exped, l * N_GROUPS + g + 1)
                    dve.wait_ge(exped, l * N_UNITS + g * GROUP + GROUP)
                    nc.vector.tensor_tensor(den[:, g % 2, :], p_sum[:, g % 2, :], sink_exp[:, g % 2, :],
                                            ALU.add).then_inc(den_made, 1)
                    dve.wait_ge(den_made, l * N_GROUPS + g + 1)
                    nc.vector.reciprocal(r_den[:, g % 2, :], den[:, g % 2, :]).then_inc(r_den_made, 1)

                def turned_low(g, c):
                    n = keys_of(g // 2)[1]
                    dve.wait_ge(pt_hi_made, l * N_UNITS + g * GROUP + c + 1)
                    src = att_bank[ATT["turned", g, c] % ATT_BANKS][:, 0:n * P].rearrange("p (k q) -> p k q", q=P)
                    nc.vector.tensor_tensor(pt_lo[:, g % 2, 0:n, c, :], src, pt_hi[:, g % 2, 0:n, c, :].bitcast(F32),
                                            ALU.subtract).then_inc(att_freed, 1)

                def evict_o(g):
                    b, kv = divmod(g, 2)
                    rows = slice(HEAD_DIM * kv, HEAD_DIM * (kv + 1))
                    dve.wait_ge(o_made, l * N_GROUPS + g + 1)
                    nc.vector.tensor_copy(y_attn[rows, :, b * P:(b + 1) * P],
                                          side_bank[rows, :].rearrange("p (c q) -> p c q", q=P)).then_inc(o_evicted, 1)

                nc.vector.memset(glu[:, :, 0:CONV_PAD], 0.0).then_inc(padded, 1)
                nc.vector.memset(glu[:, :, CONV_PAD + SEQ:], 0.0).then_inc(padded, 1)
                nc.vector.tensor_scalar(neg_sink[:], par[:, SINK:SINK + N_Q_HEADS], -1.0, None,
                                        ALU.mult).then_inc(neg_sink_made, 1)
                dve.wait_ge(padded, l * 2 + 2)
                dve.wait_ge(neg_sink_made, l + 1)
                recip(l, "mix")
                rstd_ready(l, "mix")
                tile(0)
                tile(1)
                gate(0)
                tile(2)
                taps(0, TAPS_PER_TILE)
                tile(3)
                taps(TAPS_PER_TILE, TAPS_PER_TILE)
                gate(1)
                done = 2 * TAPS_PER_TILE
                for t in range(4, 10):
                    name = IN_TILES[t]
                    if name[0] == "q":
                        c = int(name[1])
                        in_summed(t)
                        nc.vector.scalar_tensor_tensor(work[:, t % BANKS, :], bank[t % BANKS][:], q_scale[:, c:c + 1],
                                                       rstd[:], ALU.mult, ALU.mult).then_inc(evicted, 1)
                    else:
                        tile(t)
                    taps(done, TAPS_PER_TILE)
                    done += TAPS_PER_TILE
                    if name == "k":
                        low_qk(t, 0, k_hi[:], k_lo[:])
                    elif name[0] == "q":
                        low_qk(t, 1 + c, q_hi[:, c, :], q_lo[:, c, :])
                        if c == 0:
                            dve.wait_ge(v_hi_made, l + 1)
                            nc.vector.tensor_tensor(v_lo[:].rearrange("p b d -> p (b d)"), side_bank[:],
                                                    v_hi[:].rearrange("p b d -> p (b d)").bitcast(F32),
                                                    ALU.subtract).then_inc(v_split, 1)
                for c in range(GROUP):
                    bias_scores(0, c, done)
                    done += 2
                sink_args(0)
                denominators(0)
                tile(10)
                for g in range(N_GROUPS):
                    for c in range(GROUP):
                        if g + 1 < N_GROUPS:
                            bias_scores(g + 1, c, done)
                            done += 2
                        turned_low(g, c)
                    if g + 1 < N_GROUPS:
                        sink_args(g + 1)
                        denominators(g + 1)
                    if g in (1, 3):
                        tile(11 + g // 2)
                    elif g == 5:
                        tile(13, inc=3)
                    if g + 1 == N_GROUPS:
                        taps(done, TAPS_PER_GROUP)
                        done += TAPS_PER_GROUP
                    evict_o(g)
                    if g in (1, 5):
                        gate(2 + g // 4)

                for c in range(NC):
                    dve.wait_ge(y_hi_made, l * 2 * NC + c + 1)
                    nc.vector.scalar_tensor_tensor(xs_lo[:, c, :], y_attn[:, c, :], par[:, G_ATTN + c:G_ATTN + c + 1],
                                                   xs_hi[:, c, :].bitcast(F32), ALU.mult,
                                                   ALU.subtract).then_inc(y_split, 1)
                taps(done, NC * TAP_OPS - done)
                recip(l, "attn")
                rstd_ready(l, "attn")
                for m in range(ND):
                    if m >= BANKS:
                        dve.wait_ge(x_half, l * ND + m - BANKS + 1)
                    out_summed(16, m)
                    scale_tile(m % BANKS, m % BANKS)

                for c in range(NC):
                    if c == 0:
                        dve.wait_ge(stat_made, stat_no(l, "mean") + 1)
                        dve.wait_ge(tapped, (l * NC + NC) * TAP_OPS)
                    nc.vector.scalar_tensor_tensor(y_conv[:, c, :], side_bank[:], -1.0 / D_CONV, y_conv[:, c, :],
                                                   ALU.mult, ALU.add).then_inc(centred, 1)
                dve.wait_ge(centred, l * NC + NC)
                recip(l, "var")
                rstd_ready(l, "var")
                for c in range(NC):
                    dve.wait_ge(y_squared, l * 3 * NC + NC + c + 1)
                    nc.vector.tensor_tensor(y_conv[:, c, :], y_conv[:, c, :], rstd[:],
                                            ALU.mult).then_inc(ln_scaled, 1)
                for c in range(NC):
                    dve.wait_ge(y_hi_made, l * 2 * NC + NC + c + 1)
                    nc.vector.scalar_tensor_tensor(y_lo[:, c, :], y_conv[:, c, :],
                                                   par[:, G_CONV + c:G_CONV + c + 1],
                                                   y_hi[:, c, :].bitcast(F32), ALU.mult,
                                                   ALU.subtract).then_inc(y_split, 1)
                recip(l, "conv")
                rstd_ready(l, "conv")
                for m in range(ND):
                    out_summed(20, m)
                    scale_tile(m % BANKS, m % BANKS)
                    own(l, turn(OUT_C_TURN + m))
                    nc.vector.tensor_tensor(x[:, m, :], x[:, m, :], work[:, m % BANKS, :],
                                            ALU.add).then_inc(x_made, 1)
                    dve.wait_ge(x_made, l * ND + m + 1)
                    split_x(prep_no(l, 2), m, par, G_FFN2)
                ffn_steps(l, FFN_SLOTS + MIX_SLOTS, FFN_TURNS + MIX_TURNS, NF, prep_no(l, 3), "ffn2", G_NEXT)

            recip(DEPTH, "ffn1")
            rstd_ready(DEPTH, "ffn1")
            for m in range(ND):
                nc.vector.scalar_tensor_tensor(result[:, m, :], x[:, m, :], par[:, G_NEXT + m:G_NEXT + m + 1],
                                               rstd[:], ALU.mult, ALU.mult).then_inc(result_made, 1)

        @block.tensor
        def _(pe):
            pe.sem_inc(used, RING)

            def triple(to, wh, wl, mh, ml, first, last):
                nc.tensor.matmul(to, wh, mh, start=first, stop=False)
                nc.tensor.matmul(to, wh, ml, start=False, stop=False)
                return nc.tensor.matmul(to, wl, mh, start=False, stop=last)

            def weights(r, i):
                at = slice(i * P, (i + 1) * P)
                return w_hi[:, r, at], w_lo[:, r, at]

            def take(l, n):
                pe.wait_ge(split, slot_no(l, n) + 1 + RING)

            def open_bank(l, turn):
                pe.wait_ge(evicted, turn_no(l, turn) + 1)

            def statistic(l, name):
                pe.wait_ge(sq_added, l * 3 * ND + {"ffn1": ND, "mix": 2 * ND, "ffn2": 3 * ND}[name])
                nc.tensor.matmul(side_bank[:], ones[:], sq_sum[:], start=True, stop=True).then_inc(stat_made, 1)

            def statistic_of(l, to, ready, base, chunks):
                for c in range(NC):
                    pe.wait_ge(ready, base + (c + 1))
                    last = nc.tensor.matmul(to, ones[:], chunks[:, c, :], start=c == 0, stop=c == NC - 1)
                last.then_inc(stat_made, 1)

            def model_tile(l, n, r, turn, b, prep=None, part=(0, ND)):
                first, end = part
                take(l, n)
                if first == 0:
                    open_bank(l, turn)
                for k in range(first, end):
                    if prep is not None:
                        pe.wait_ge(x_split, prep * ND + k + 1)
                    last = triple(bank[b][:], *weights(r, k - first), xs_hi[:, k, :], xs_lo[:, k, :], k == 0,
                                  k == ND - 1)
                last.then_inc(used, 1)

            def ffn_steps(l, base, turns, h_base, prep, name):
                for j in range(4):
                    model_tile(l, base + j, j, turns + j, j, prep if j == 0 else None)
                    if j == 0:
                        statistic(l, name)
                with pe.Fori(1, NF // 2) as i:
                    for j in range(4):
                        model_tile(l, base + i * 4 + j, j, turns + i * 4 + j, j)
                with pe.Fori(0, ND // 4) as i:
                    for j in range(4):
                        turn = turns + 2 * NF + i * 4 + j
                        open_bank(l, turn)
                        f = 0
                        for s, count in enumerate(DOWN):
                            take(l, base + 2 * NF + (i * 4 + j) * 4 + s)
                            pe.wait_ge(h_split, l * 2 * NF + h_base + f + count)
                            for k in range(count):
                                last = triple(bank[j][:], *weights(s, k), h_hi[:, f, :], h_lo[:, f, :], f == 0,
                                              f == NF - 1)
                                f += 1
                            last.then_inc(used, 1)

            pe.wait_ge(consts_v, 1)
            pe.wait_ge(consts_p, 3)
            with pe.Fori(0, DEPTH) as l:
                ffn_steps(l, 0, 0, 0, prep_no(l, 0), "ffn1")

                def in_tile(t):
                    if t < 12:
                        model_tile(l, MIX_S + t, t % RING, MIX_T + t, t % BANKS, prep_no(l, 1) if t == 0 else None)
                    else:
                        for half in range(2):
                            s = 12 + 2 * (t - 12) + half
                            model_tile(l, MIX_S + s, s % RING, MIX_T + t, t % BANKS,
                                       part=(4 * half, 4 * half + 4))

                def scores(g, c):
                    b, kv = divmod(g, 2)
                    first, n = keys_of(b)
                    k = ATT["scores", g, c]
                    rows = slice(HEAD_DIM * kv, HEAD_DIM * (kv + 1))
                    q, keys = slice(b * P, (b + 1) * P), slice(first * P, (first + n) * P)
                    to = att_bank[k % ATT_BANKS][:, 0:n * P]
                    if k >= ATT_BANKS:
                        pe.wait_ge(att_freed, l * len(ATT) + k - ATT_BANKS + 1)
                    nc.tensor.matmul(to, q_hi[rows, c, q], k_hi[rows, keys], start=True, stop=False)
                    nc.tensor.matmul(to, q_hi[rows, c, q], k_lo[rows, keys], start=False, stop=False)
                    nc.tensor.matmul(to, q_lo[rows, c, q], k_hi[rows, keys], start=False,
                                     stop=True).then_inc(scored, 1)

                def turn_weights(g, c):
                    n = keys_of(g // 2)[1]
                    k = ATT["turned", g, c]
                    pe.wait_ge(normed, l * N_UNITS + g * GROUP + c + 1)
                    pe.wait_ge(att_freed, l * len(ATT) + k - ATT_BANKS + 1)
                    for i in range(n):
                        last = nc.tensor.transpose(att_bank[k % ATT_BANKS][:, i * P:(i + 1) * P],
                                                   prob[:, g % 2, c, i * P:(i + 1) * P], ident[:])
                    last.then_inc(turned, 1)

                def weigh_values(g):
                    first, n = keys_of(g // 2)
                    pe.wait_ge(att_freed, l * len(ATT) + ATT["turned", g, GROUP - 1] + 1)
                    if g:
                        pe.wait_ge(o_evicted, l * N_GROUPS + g)
                    for i in range(n):
                        mh = pt_hi[:, g % 2, i, :, :].rearrange("p c q -> p (c q)")
                        ml = pt_lo[:, g % 2, i, :, :].rearrange("p c q -> p (c q)")
                        last = triple(side_bank[:], v_hi[:, first + i, :], v_lo[:, first + i, :], mh, ml, i == 0,
                                      i == n - 1)
                    last.then_inc(o_made, 1)

                def out_tiles(first_slot, first_turn, hi, lo, done, stat):
                    for m in range(ND):
                        s = first_slot + m // 2
                        if m % 2 == 0:
                            take(l, MIX_S + s)
                        open_bank(l, MIX_T + first_turn + m)
                        for c in range(NC):
                            if m == 0:
                                pe.wait_ge(y_split, l * 2 * NC + done + c + 1)
                            last = triple(bank[m % BANKS][:], *weights(s % RING, 4 * (m % 2) + c),
                                          hi[:, c, :], lo[:, c, :], c == 0, c == NC - 1)
                        last.then_inc(used if m % 2 else half_used, 1)
                        if m == 0:
                            stat()

                in_tile(0)
                statistic(l, "mix")
                for t in range(1, 7):
                    in_tile(t)
                pe.wait_ge(evicted, turn_no(l, MIX_T + IN_TILES.index("v")) + 1 + BANKS)
                pe.wait_ge(std_made, root_no(l, "mix") + 1)
                for b in range(NB):
                    last = nc.tensor.transpose(side_bank[:, b * P:(b + 1) * P],
                                               work[:, IN_TILES.index("v") % BANKS, b * P:(b + 1) * P], ident[:])
                last.then_inc(v_turned, 1)
                for t in range(7, 10):
                    in_tile(t)
                pe.wait_ge(qk_split, l * (NC + 1) + NC + 1)
                pe.wait_ge(v_split, l + 1)
                for c in range(GROUP):
                    scores(0, c)
                in_tile(10)
                for g in range(N_GROUPS):
                    for c in range(GROUP):
                        if g + 1 < N_GROUPS:
                            scores(g + 1, c)
                        turn_weights(g, c)
                    weigh_values(g)
                    if g in (0, 2, 4):
                        in_tile(11 + g // 2)

                def attn_stat():
                    pe.wait_ge(o_evicted, l * N_GROUPS + N_GROUPS)
                    statistic_of(l, side_bank[:], y_squared, l * 3 * NC, work)

                out_tiles(16, OUT_A_TURN, xs_hi, xs_lo, 0, attn_stat)
                pe.wait_ge(std_made, root_no(l, "attn") + 1)
                for c in range(NC):
                    pe.wait_ge(tapped, (l * NC + c + 1) * TAP_OPS)
                    last = nc.tensor.matmul(side_bank[:], ones[:], y_conv[:, c, :], start=c == 0, stop=c == NC - 1)
                last.then_inc(stat_made, 1)
                statistic_of(l, att_bank[2][:], y_squared, l * 3 * NC + NC, work)

                def conv_stat():
                    statistic_of(l, side_bank[:], y_squared, l * 3 * NC + 2 * NC, work)

                out_tiles(20, OUT_C_TURN, y_hi, y_lo, NC, conv_stat)
                ffn_steps(l, FFN_SLOTS + MIX_SLOTS, FFN_TURNS + MIX_TURNS, NF, prep_no(l, 2), "ffn2")
            pe.wait_ge(sq_added, (DEPTH * 3 + 1) * ND)
            nc.tensor.matmul(side_bank[:], ones[:], sq_sum[:], start=True, stop=True).then_inc(stat_made, 1)


def by_partition(v):
    return v.reshape(v.shape[0], -1, P).transpose(0, 2, 1)


def tiles_of(w, n_out):
    *lead, k, n = w.shape
    w = w.reshape(*lead, k // P, P, n // n_out, n_out)
    d = len(lead)
    w = w.transpose(*range(d), d + 2, d + 1, d, d + 3)
    return w.reshape(*lead, n // n_out, P, k // P * n_out)


def heads_paired(v, axis):
    shape = v.shape
    v = v.reshape(*shape[:axis], N_KV_HEADS, GROUP, HEAD_DIM, *shape[axis + 1:])
    return v.swapaxes(axis, axis + 1).reshape(shape)


def kernel(**inputs):
    import concourse.bacc as bacc
    from concourse.bass_utils import run_bass_kernel_spmd

    a = {k: np.asarray(v) for k, v in inputs.items()}
    next_norm = np.concatenate([a["ffn1_norm"][1:], a["final_norm"][None]], axis=0)
    conv_w = a["conv_w"].transpose(0, 2, 1).reshape(DEPTH, NC, P, CONV_WIDTH).transpose(0, 2, 1, 3)
    params = np.concatenate([
        by_partition(a["mix_norm"]), by_partition(a["ffn2_norm"]), by_partition(next_norm),
        conv_w.reshape(DEPTH, P, NC * CONV_WIDTH), by_partition(a["conv_b"]), by_partition(a["conv_ln_g"]),
        by_partition(a["conv_ln_b"]), by_partition(a["out_norm_conv"]),
        by_partition(heads_paired(a["out_norm_attn"], 1)),
        np.broadcast_to(a["attn_sink"][:, None, :], (DEPTH, P, N_Q_HEADS)),
    ], axis=2)

    def gate_up(ffn):
        both = np.stack([tiles_of(a[f"{ffn}_w_gate"], P), tiles_of(a[f"{ffn}_w_up"], P)], axis=2)
        return both.reshape(DEPTH, 2 * NF, P, 8 * P)

    w_in = a["w_in"]
    conv_in, q_in, kv_in = w_in[..., :2 * D_CONV], w_in[..., 2 * D_CONV:3 * D_CONV], w_in[..., 3 * D_CONV:]
    in_tiles = tiles_of(np.concatenate([conv_in, heads_paired(q_in, 2), kv_in], axis=2), P)
    order = {"a": 0, "g": NC, "q": 2 * NC, "k": 3 * NC, "v": 3 * NC + 1}
    in_order = [order[t[0]] + int(t[1:] or 0) for t in IN_TILES]
    w_out = a["w_out"]
    out_a = tiles_of(heads_paired(w_out[:, D_CONV:], 1), P)
    out_c = tiles_of(w_out[:, :D_CONV], P)
    pair = [t.reshape(DEPTH, ND // 2, 2, P, 4 * P).transpose(0, 1, 3, 2, 4).reshape(DEPTH, ND // 2, P, 8 * P)
            for t in (out_a, out_c)]
    arrays = {
        "xT": a["x"].reshape(SEQ, D_MODEL).T,
        "first_gain": by_partition(a["ffn1_norm"])[0],
        "params": params,
        "w_gu": np.stack([gate_up("ffn1"), gate_up("ffn2")], axis=1),
        "w_down": np.stack([tiles_of(a["ffn1_w_down"], P), tiles_of(a["ffn2_w_down"], P)], axis=1),
        "w_in": in_tiles[:, in_order],
        "w_out": np.concatenate(pair, axis=1),
    }
    arrays = {k: np.ascontiguousarray(v) for k, v in arrays.items()}
    nc = bacc.Bacc("TRN2", target_bir_lowering=False, num_devices=1)
    args = [nc.dram_tensor(k, v.shape, mybir.dt.from_np(v.dtype), kind="ExternalInput").ap()
            for k, v in arrays.items()]
    out = nc.dram_tensor("out", (D_MODEL, SEQ), F32, kind="ExternalOutput").ap()
    encoder(nc, *args, out)
    r = run_bass_kernel_spmd(nc, [arrays], core_ids=[0])
    return np.ascontiguousarray(r.results[0]["out"].T).reshape(1, SEQ, D_MODEL)
```

```python
import math
from contextlib import ExitStack

import numpy as np

import concourse.bass as bass
from concourse import mybir

P = 128
D_MODEL, SEQ, DEPTH, D_FF = 1024, 512, 2, 2816
D_CONV, CONV_WIDTH, HEAD_DIM = 512, 31, 64
N_Q_HEADS, N_KV_HEADS = 8, 2
GROUP = N_Q_HEADS // N_KV_HEADS
CONV_PAD = CONV_WIDTH // 2
EPS = 1e-6
MASKED = 1e30

ND = D_MODEL // P
NF = D_FF // P
NC = D_CONV // P
NB = SEQ // P
RING = 4
BANKS = 4
DOWN = (6, 6, 5, 5)
assert sum(DOWN) == NF

IN_TILES = ["a0", "g0", "a1", "g1", "a2", "g2", "k", "v", "q0", "q1", "q2", "q3", "a3", "g3"]
IN_SLOTS = [(t,) for t in range(12)] + [(12, 0), (12, 1), (13, 0), (13, 1)]

FFN_SLOTS, MIX_SLOTS = 2 * NF + 4 * ND, 24
LAYER_SLOTS = 2 * FFN_SLOTS + MIX_SLOTS
FFN_TURNS, MIX_TURNS = 2 * NF + ND, 32
LAYER_TURNS = 2 * FFN_TURNS + MIX_TURNS
OUT_A_TURN, OUT_C_TURN = 16, 24
assert LAYER_SLOTS % RING == 0 and LAYER_TURNS % BANKS == 0

STATS = ["ffn1", "mix", "attn", "mean", "var", "conv", "ffn2"]
ROOTS = [s for s in STATS if s != "mean"]

G_MIX, G_FFN2, G_NEXT = 0, 8, 16
CONV_W = 24
CONV_B = CONV_W + NC * CONV_WIDTH
LN_G, LN_B, G_CONV, G_ATTN = CONV_B + 4, CONV_B + 8, CONV_B + 12, CONV_B + 16
SINK = CONV_B + 20
N_PAR = SINK + N_Q_HEADS

ALU = mybir.AluOpType
ACT = mybir.ActivationFunctionType
F32 = mybir.dt.float32
F32R = mybir.dt.float32r
I32 = mybir.dt.int32


def keys_of(b):
    first = max(0, b - 1)
    return first, min(NB, b + 2) - first


def slope(kv, c):
    return 2.0 ** (-8.0 * (kv * GROUP + c + 1) / N_Q_HEADS)


AHEAD = 2
PROBS = AHEAD + 1


def attention_turns():
    turns = [("scores", g, c) for g in range(AHEAD) for c in range(GROUP)]
    for g in range(2 * NB):
        for c in range(GROUP):
            turns.append(("turned", g, c))
            if g + AHEAD < 2 * NB:
                turns.append(("scores", g + AHEAD, c))
    return {use: n for n, use in enumerate(turns)}


ATT = attention_turns()
ATT_BANKS = 6
N_GROUPS = 2 * NB
N_UNITS = N_GROUPS * GROUP
V_TAPS = 20
P_TAPS = CONV_WIDTH - V_TAPS
V_OPS = V_TAPS + 1
V_SPREAD = [5] * 8 + [6] * 2
P_SPREAD = [2] * 10 + [3] * 8
MERGED_AT = [(0, 0), (3, 2), (7, 1)]
assert sum(V_SPREAD) + 4 * N_GROUPS == NC * V_OPS and sum(P_SPREAD) == NC * P_TAPS


def encoder(nc, xT, first_gain, params, w_gu, w_down, w_in, w_out, out):
    with ExitStack() as ctx:
        def sb(name, shape, dt=F32, stack=ctx):
            return stack.enter_context(nc.sbuf_tensor(name, shape, dt))

        def sem(name):
            return ctx.enter_context(nc.semaphore(name))

        x = sb("x", [P, ND, SEQ])
        xs_hi = sb("xs_hi", [P, ND, SEQ], F32R)
        xs_lo = sb("xs_lo", [P, ND, SEQ], F32R)
        stage = sb("stage", [P, RING, 8 * P])
        w_hi = sb("w_hi", [P, RING, 8 * P], F32R)
        w_lo = sb("w_lo", [P, RING, 8 * P], F32R)
        work = sb("work", [P, BANKS, SEQ])
        sq = sb("sq", [P, SEQ])
        sq_sum = sb("sq_sum", [P, SEQ])
        zero = sb("zero", [P, 1])
        pool_taps = sb("pool_taps", [P, SEQ])
        std = sb("std", [P, SEQ])
        rstd = sb("rstd", [P, SEQ])
        dist = sb("dist", [P, 3 * P])
        ident = sb("ident", [P, P])
        ones = sb("ones", [P, P])
        q_scale = sb("q_scale", [P, NC])
        eps = sb("eps", [P, 1])
        gain0 = sb("gain0", [P, ND])
        par = sb("par", [P, N_PAR])
        neg_sink = sb("neg_sink", [P, N_Q_HEADS])
        neg_max = sb("neg_max", [P, PROBS, GROUP])
        p_sum = sb("p_sum", [P, PROBS, GROUP])
        sink_arg = sb("sink_arg", [P, PROBS, GROUP])
        sink_exp = sb("sink_exp", [P, PROBS, GROUP])
        den = sb("den", [P, PROBS, GROUP])
        r_den = sb("r_den", [P, PROBS, GROUP])

        with ExitStack() as region:
            h_hi = sb("h_hi", [P, NF, SEQ], F32R, region)
            h_lo = sb("h_lo", [P, NF, SEQ], F32R, region)
        with ExitStack() as region:
            prob = sb("prob", [P, 2, GROUP, 3 * P], F32, region)
            pt_hi = sb("pt_hi", [P, 2, 3, GROUP, P], F32R, region)
            pt_lo = sb("pt_lo", [P, 2, 3, GROUP, P], F32R, region)
            glu = sb("glu", [P, NC, SEQ + 2 * CONV_PAD], F32, region)
            y_conv = sb("y_conv", [P, NC, SEQ], F32, region)
            odd_taps = sb("odd_taps", [P, SEQ], F32, region)
            q_hi = sb("q_hi", [P, NC, SEQ], F32R, region)
            q_lo = sb("q_lo", [P, NC, SEQ], F32R, region)
            k_hi = sb("k_hi", [P, SEQ], F32R, region)
            k_lo = sb("k_lo", [P, SEQ], F32R, region)
            v_hi = sb("v_hi", [P, NB, P], F32R, region)
            v_lo = sb("v_lo", [P, NB, P], F32R, region)
            y_attn = sb("y_attn", [P, NC, SEQ], F32, region)
        probs = [prob[:, i] for i in range(2)]
        probs.append(work[:].rearrange("p m n -> p (m n)")[:, 0:GROUP * 3 * P]
                     .rearrange("p (c n) -> p c n", c=GROUP))
        squares = prob[:].rearrange("p a c n -> p (a c n)")[:, 0:NC * SEQ].rearrange("p (c n) -> p c n", c=NC)
        product = [sq, sq_sum]
        y_hi, y_lo = q_hi, q_lo
        with ExitStack() as region:
            result = sb("result", [P, ND, SEQ], F32, region)
            dist_int = sb("dist_int", [P, 3 * P], I32, region)
            dist_neg = sb("dist_neg", [P, 3 * P], F32, region)
        x_squares = result

        bank = [ctx.enter_context(nc.psum_tensor(f"bank{i}", [P, SEQ], F32)) for i in range(8)]
        att_bank, side_bank = bank[4:7] + [bank[0], bank[2], bank[3]], bank[7]

        landed = [sem(f"landed{i}") for i in range(RING)]
        gain_landed = sem("gain_landed")
        x_landed = [sem(f"x_landed{i}") for i in range(4)]
        par_landed = sem("par_landed")
        hi_made = sem("hi_made")
        split = sem("split")
        used = sem("used")
        half_used = sem("half_used")
        evicted = sem("evicted")
        silu_made = sem("silu_made")
        h_made = sem("h_made")
        h_hi_made = sem("h_hi_made")
        h_split = sem("h_split")
        x_made = sem("x_made")
        x_half = sem("x_half")
        x_hi_made = sem("x_hi_made")
        x_split = sem("x_split")
        squared = sem("squared")
        sq_added = sem("sq_added")
        stat_made = sem("stat_made")
        std_made = sem("std_made")
        rstd_made = sem("rstd_made")
        consts_v = sem("consts_v")
        consts_p = sem("consts_p")
        small_made = sem("small_made")
        padded = sem("padded")
        sig_made = sem("sig_made")
        glu_made = sem("glu_made")
        tapped = sem("tapped")
        tap_product = sem("tap_product")
        tap_added = sem("tap_added")
        taps_merged = sem("taps_merged")
        qk_hi = sem("qk_hi")
        qk_split = sem("qk_split")
        v_turned = sem("v_turned")
        v_hi_made = sem("v_hi_made")
        v_split = sem("v_split")
        scored = sem("scored")
        att_freed = sem("att_freed")
        exped = sem("exped")
        sink_ready = sem("sink_ready")
        sink_exped = sem("sink_exped")
        den_made = sem("den_made")
        r_den_made = sem("r_den_made")
        normed_a = sem("normed_a")
        normed_p = sem("normed_p")
        turned = sem("turned")
        pt_hi_made = sem("pt_hi_made")
        o_made = sem("o_made")
        o_evicted = sem("o_evicted")
        y_hi_made = sem("y_hi_made")
        y_split = sem("y_split")
        y_squared = sem("y_squared")
        centred = sem("centred")
        ln_scaled = sem("ln_scaled")
        ln_silu = sem("ln_silu")
        neg_sink_made = sem("neg_sink_made")
        result_made = sem("result_made")
        stored = sem("stored")

        def slot_no(l, n):
            return l * LAYER_SLOTS + n

        def turn_no(l, n):
            return l * LAYER_TURNS + n

        def stat_no(l, name):
            return l * len(STATS) + STATS.index(name)

        def root_no(l, name):
            return l * len(ROOTS) + ROOTS.index(name)

        def prep_no(l, which):
            return l * 3 + which

        def chunk(t, m):
            return t[:, m, :] if isinstance(m, int) else t[:, bass.ds(m, 1), :].rearrange("p o n -> p (o n)")

        def column(t, m):
            return t[:, m:m + 1] if isinstance(m, int) else t[:, bass.ds(m, 1)]

        FFNS = [(0, 0, 0, 0, "ffn1"), (FFN_SLOTS + MIX_SLOTS, FFN_TURNS + MIX_TURNS, NF, 2, "ffn2")]
        MIX_S, MIX_T = FFN_SLOTS, FFN_TURNS
        ln_rstd = pool_taps
        stat_bank = {"attn": side_bank, "mean": att_bank[0], "var": att_bank[1], "conv": att_bank[2]}

        block = ctx.enter_context(nc.Block())

        @block.sync
        def _(sp):
            sp.dma_start(gain0[:], first_gain).then_inc(gain_landed, 16)
            for i in range(4):
                sp.dma_start(x[:, 2 * i:2 * i + 2, :],
                             xT.rearrange("(k p) n -> p k n", p=P)[:, 2 * i:2 * i + 2, :]).then_inc(x_landed[i], 16)

            def load(l, n, r, src, width):
                sp.wait_ge(split, slot_no(l, n) + 1)
                sp.dma_start(stage[:, r, 0:width], src).then_inc(landed[r], 16)

            def ffn_loads(l, which, base):
                with sp.Fori(0, 2 * NF // RING) as i:
                    for j in range(RING):
                        src = w_gu[bass.ds(l, 1), which, bass.ds(i * RING + j, 1)]
                        load(l, base + i * RING + j, j, src.rearrange("o t p n -> p (o t n)"), 8 * P)
                if which == 0:
                    sp.wait_ge(x_split, prep_no(l, 0) * ND + ND)
                    sp.dma_start(par[:], params[bass.ds(l, 1)].rearrange("o p n -> p (o n)")).then_inc(par_landed, 16)
                with sp.Fori(0, ND) as m:
                    at = 0
                    for j, count in enumerate(DOWN):
                        src = w_down[bass.ds(l, 1), which, bass.ds(m, 1), :, at:at + count * P]
                        load(l, base + 2 * NF + m * 4 + j, j, src.rearrange("o t p n -> p (o t n)"), count * P)
                        at += count * P

            with sp.Fori(0, DEPTH) as l:
                ffn_loads(l, 0, 0)
                for s, (t, *half) in enumerate(IN_SLOTS):
                    width = 4 * P if half else 8 * P
                    start = 4 * P * half[0] if half else 0
                    src = w_in[bass.ds(l, 1), t, :, start:start + width].rearrange("o p n -> p (o n)")
                    load(l, MIX_S + s, s % RING, src, width)
                for s in range(8):
                    src = w_out[bass.ds(l, 1), s].rearrange("o p n -> p (o n)")
                    load(l, MIX_S + 16 + s, s % RING, src, 8 * P)
                ffn_loads(l, 1, FFN_SLOTS + MIX_SLOTS)

            out_v = out.rearrange("(k p) n -> p k n", p=P)
            for m in range(ND):
                sp.wait_ge(result_made, m + 1)
                sp.dma_start(out_v[:, m, :], result[:, m, :]).then_inc(stored, 16)
            sp.wait_ge(stored, 16 * ND)

        @block.gpsimd
        def _(pool):
            pool.sem_inc(split, RING)
            nc.gpsimd.iota(dist_int[:], pattern=[[-1, 3 * P]], base=P, channel_multiplier=1).then_inc(consts_p, 1)
            nc.gpsimd.memset(ident[:], 0.0).then_inc(consts_p, 1)
            pool.wait_ge(consts_p, 2)
            nc.gpsimd.affine_select(out=ident[:], in_=ident[:], compare_op=ALU.not_equal, fill=1.0, base=0,
                                    pattern=[[-1, P]], channel_multiplier=1).then_inc(consts_p, 1)
            pool.wait_ge(consts_v, 3)
            nc.gpsimd.affine_select(out=dist[:], in_=dist[:], compare_op=ALU.is_ge, fill=MASKED, base=0,
                                    pattern=[[1, 3 * P]], channel_multiplier=-1).then_inc(consts_p, 1)
            pool.wait_ge(consts_p, 4)
            nc.gpsimd.affine_select(out=dist[:], in_=dist[:], compare_op=ALU.is_ge, fill=MASKED, base=2 * P,
                                    pattern=[[-1, 3 * P]], channel_multiplier=1).then_inc(consts_p, 1)

            def low(l, n, r):
                pool.wait_ge(hi_made, slot_no(l, n) + 1)
                nc.gpsimd.tensor_tensor(w_lo[:, r, :], stage[:, r, :], w_hi[:, r, :].bitcast(F32),
                                        ALU.subtract).then_inc(split, 1)

            def add_square(prep, m, first=False):
                pool.wait_ge(squared, prep * ND + m + 1)
                if not first:
                    pool.wait_ge(sq_added, prep * ND + m)
                start = zero[:, 0:1].to_broadcast([P, SEQ])
                nc.gpsimd.tensor_tensor(sq_sum[:], start if first else sq_sum[:], sq[:],
                                        ALU.add).then_inc(sq_added, 1)

            def ffn_steps(l, base, next_prep, last):
                with pool.Fori(0, NF // 2) as i:
                    for j in range(4):
                        low(l, base + i * 4 + j + RING, j)
                at = base + 2 * NF
                for j in range(4):
                    low(l, at + RING + j, j)
                add_square(next_prep, 0, first=True)
                with pool.Fori(1, ND - 1) as m:
                    for j in range(4):
                        low(l, at + m * 4 + RING + j, j)
                    add_square(next_prep, m)
                if not last:
                    for j in range(4):
                        low(l, at + ND * 4 + j, j)
                add_square(next_prep, ND - 1)

            pool.wait_ge(small_made, 1)
            with pool.Fori(0, DEPTH) as l:
                for j in range(RING):
                    low(l, j, j)
                ffn_steps(l, 0, prep_no(l, 1), last=False)

                def mix_low(s):
                    low(l, MIX_S + s + RING, s % RING)

                def add_products(first, count):
                    for n in range(first, first + count):
                        c, t = divmod(n, P_TAPS)
                        if n:
                            pool.wait_ge(tap_added, l * NC * P_TAPS + n)
                        if t == 0 and c:
                            pool.wait_ge(taps_merged, l * NC + c)
                        pool.wait_ge(tap_product, l * NC * P_TAPS + n + 1)
                        start = zero[:, 0:1].to_broadcast([P, SEQ])
                        nc.gpsimd.tensor_tensor(pool_taps[:], start if t == 0 else pool_taps[:], product[n % 2][:],
                                                ALU.add).then_inc(tap_added, 1)

                def normalise(g):
                    n = keys_of(g // 2)[1] * P
                    for c in range(GROUP // 2, GROUP):
                        unit = probs[g % PROBS][:, c, 0:n]
                        pool.wait_ge(exped, l * N_UNITS + g * GROUP + c + 1)
                        pool.wait_ge(r_den_made, l * N_GROUPS + g + 1)
                        nc.gpsimd.tensor_tensor(unit, unit, r_den[:, g % PROBS, c:c + 1].to_broadcast([P, n]),
                                                ALU.mult).then_inc(normed_p, 1)

                done = 0
                for t in range(12):
                    mix_low(t)
                    if t >= 2:
                        add_products(done, P_SPREAD[t - 2])
                        done += P_SPREAD[t - 2]
                mix_low(12)
                mix_low(13)
                normalise(0)
                mix_low(14)
                mix_low(15)
                add_products(done, P_SPREAD[10])
                done += P_SPREAD[10]
                for g in range(N_GROUPS - 1):
                    normalise(g + 1)
                    add_products(done, P_SPREAD[11 + g])
                    done += P_SPREAD[11 + g]
                for s in range(4):
                    low(l, MIX_S + 16 + s + RING, s % RING)
                    for m in (2 * s, 2 * s + 1):
                        pool.wait_ge(evicted, turn_no(l, MIX_T + OUT_A_TURN + m) + 1 + BANKS)
                        nc.gpsimd.tensor_tensor(x[:, m, :], x[:, m, :], work[:, m % BANKS, :],
                                                ALU.add).then_inc(x_half, 1)
                for s in range(4):
                    low(l, MIX_S + 20 + s + RING, s % RING)
                    for m in (2 * s, 2 * s + 1):
                        add_square(prep_no(l, 2), m, first=m == 0)
                ffn_steps(l, FFN_SLOTS + MIX_SLOTS, prep_no(l, 3), last=True)

        @block.scalar
        def _(act):
            def high(l, n, r, uses):
                act.wait_ge(landed[r], uses * 16 + 16)
                act.wait_ge(used, slot_no(l, n) + 1)
                nc.scalar.activation(w_hi[:, r, :], stage[:, r, :], ACT.Copy).then_inc(hi_made, 1)

            def uses_of(l, n, r):
                return l * (LAYER_SLOTS // RING) + n

            def prepare(prep, m, gain, gain_at):
                nc.scalar.activation(xs_hi[:, m, :], x[:, m, :], ACT.Copy,
                                     scale=gain[:, gain_at + m:gain_at + m + 1]).then_inc(x_hi_made, 1)
                act.wait_ge(sq_added, prep * ND + m)
                nc.scalar.activation(sq[:], x[:, m, :], ACT.Square).then_inc(squared, 1)

            def root(l, name, source, count):
                act.wait_ge(stat_made, stat_no(l, name) + 1)
                act.wait_ge(rstd_made, root_no(l, name) + 1)
                nc.scalar.activation(std[:], source[:], ACT.Sqrt, bias=eps[:], scale=1.0 / count).then_inc(std_made, 1)

            def ffn_steps(l, base, turns, name, last):
                root(l, name, side_bank, D_MODEL)
                with act.Fori(0, NF // 2) as i:
                    for j in range(2):
                        f = i * 2 + j
                        high(l, base + f * 2 + RING, 2 * j, uses_of(l, base // RING + 1 + i, 0))
                        act.wait_ge(evicted, turn_no(l, turns + f * 2) + 1 + BANKS)
                        nc.scalar.activation(work[:, 2 * j, :], work[:, 2 * j, :], ACT.Silu).then_inc(silu_made, 1)
                        high(l, base + f * 2 + 1 + RING, 2 * j + 1, uses_of(l, base // RING + 1 + i, 0))
                at = base + 2 * NF

                def down(m):
                    for j in range(4):
                        high(l, at + m * 4 + RING + j, j, uses_of(l, at // RING + 1 + m, 0))

                with act.Fori(0, ND - 1) as m:
                    down(m)
                if not last:
                    down(ND - 1)

            act.wait_ge(small_made, 1)
            for m in range(ND):
                if m % 2 == 0:
                    act.wait_ge(x_landed[m // 2], 16)
                nc.scalar.activation(x_squares[:, m, :], x[:, m, :], ACT.Square).then_inc(squared, 1)
            with act.Fori(0, DEPTH) as l:
                for j in range(RING):
                    high(l, j, j, uses_of(l, 0, 0))
                ffn_steps(l, 0, 0, "ffn1", last=False)

                def mix_high(s):
                    high(l, MIX_S + s + RING, s % RING, uses_of(l, (MIX_S + s) // RING + 1, 0))

                def tile_ready(t):
                    act.wait_ge(evicted, turn_no(l, MIX_T + t) + 1 + BANKS)

                def sigmoid(c, t):
                    tile_ready(t)
                    nc.scalar.activation(work[:, t % BANKS, :], work[:, t % BANKS, :],
                                         ACT.Sigmoid).then_inc(sig_made, 1)

                def exp_scores(g, c):
                    b, kv = divmod(g, 2)
                    n = keys_of(b)[1] * P
                    unit = probs[g % PROBS][:, c, 0:n]
                    act.wait_ge(att_freed, l * len(ATT) + ATT["scores", g, c] + 1)
                    nc.scalar.activation(unit, unit, ACT.Exp, bias=neg_max[:, g % PROBS, c:c + 1], scale=-1.0,
                                         accum_out=p_sum[:, g % PROBS, c:c + 1]).then_inc(exped, 1)

                def exp_sink(g):
                    act.wait_ge(sink_ready, l * N_GROUPS + g + 1)
                    nc.scalar.activation(sink_exp[:, g % PROBS, :], sink_arg[:, g % PROBS, :], ACT.Exp).then_inc(sink_exped, 1)

                def normalise(g):
                    act.wait_ge(r_den_made, l * N_GROUPS + g + 1)
                    act.wait_ge(exped, l * N_UNITS + g * GROUP + GROUP)
                    for c in range(GROUP // 2):
                        unit = probs[g % PROBS][:, c, 0:keys_of(g // 2)[1] * P]
                        nc.scalar.activation(unit, unit, ACT.Copy, scale=r_den[:, g % PROBS, c:c + 1]).then_inc(normed_a, 1)

                def products(first, count):
                    for n in range(first, first + count):
                        c, t = n // P_TAPS, V_TAPS + n % P_TAPS
                        if n >= 2:
                            act.wait_ge(tap_added, l * NC * P_TAPS + n - 1)
                        act.wait_ge(glu_made, l * NC + c + 1)
                        at = CONV_W + c * CONV_WIDTH + t
                        nc.scalar.activation(product[n % 2][:], glu[:, c, t:t + SEQ], ACT.Copy,
                                             scale=par[:, at:at + 1]).then_inc(tap_product, 1)

                def turned_high(g, c):
                    n = keys_of(g // 2)[1]
                    act.wait_ge(turned, l * N_UNITS + g * GROUP + c + 1)
                    if g >= 2 and c == 0:
                        act.wait_ge(o_made, l * N_GROUPS + g - 1)
                    src = att_bank[ATT["turned", g, c] % ATT_BANKS][:, 0:n * P].rearrange("p (k q) -> p k q", q=P)
                    nc.scalar.activation(pt_hi[:, g % 2, 0:n, c, :], src, ACT.Copy).then_inc(pt_hi_made, 1)

                root(l, "mix", side_bank, D_MODEL)
                done = 0
                for t in range(12):
                    mix_high(t)
                    name = IN_TILES[t]
                    if name[0] == "g":
                        sigmoid(int(name[1]), t)
                    elif name == "k":
                        tile_ready(t)
                        nc.scalar.activation(k_hi[:], work[:, t % BANKS, :], ACT.Copy).then_inc(qk_hi, 1)
                    elif name[0] == "q":
                        c = int(name[1])
                        tile_ready(t)
                        nc.scalar.activation(q_hi[:, c, :], work[:, t % BANKS, :], ACT.Copy).then_inc(qk_hi, 1)
                        if c == 0:
                            act.wait_ge(v_turned, l + 1)
                            nc.scalar.activation(v_hi[:].rearrange("p b d -> p (b d)"), side_bank[:],
                                                 ACT.Copy).then_inc(v_hi_made, 1)
                    if t >= 2:
                        products(done, P_SPREAD[t - 2])
                        done += P_SPREAD[t - 2]
                mix_high(12)
                mix_high(13)
                for c in range(GROUP):
                    exp_scores(0, c)
                exp_sink(0)
                normalise(0)
                mix_high(14)
                mix_high(15)
                for c in range(GROUP):
                    exp_scores(1, c)
                exp_sink(1)
                products(done, P_SPREAD[10])
                done += P_SPREAD[10]
                sigmoid(3, 13)
                for g in range(N_GROUPS):
                    p = P_SPREAD[11 + g] if g + 1 < N_GROUPS else 0
                    for c in range(GROUP):
                        turned_high(g, c)
                        if c and g + AHEAD < N_GROUPS:
                            exp_scores(g + AHEAD, c - 1)
                        elif c == 0 and g and g + 1 < N_GROUPS:
                            exp_scores(g + 1, GROUP - 1)
                            exp_sink(g + 1)
                        if c == 2 and g + 1 < N_GROUPS:
                            normalise(g + 1)
                        elif p:
                            products(done, 1)
                            done += 1

                for c in range(NC):
                    if c == 0:
                        act.wait_ge(o_evicted, l * N_GROUPS + N_GROUPS)
                    nc.scalar.activation(xs_hi[:, c, :], y_attn[:, c, :], ACT.Copy,
                                         scale=par[:, G_ATTN + c:G_ATTN + c + 1]).then_inc(y_hi_made, 1)
                for c in range(NC):
                    nc.scalar.activation(squares[:, c, :], y_attn[:, c, :], ACT.Square).then_inc(y_squared, 1)
                root(l, "attn", stat_bank["attn"], D_CONV)
                mix_high(16)
                for c in range(NC):
                    act.wait_ge(centred, l * NC + c + 1)
                    nc.scalar.activation(squares[:, c, :], y_conv[:, c, :], ACT.Square).then_inc(y_squared, 1)
                mix_high(17)
                root(l, "var", stat_bank["var"], D_CONV)
                for c in range(NC):
                    act.wait_ge(ln_scaled, l * NC + c + 1)
                    nc.scalar.activation(y_conv[:, c, :], y_conv[:, c, :], ACT.Silu,
                                         bias=par[:, LN_B + c:LN_B + c + 1],
                                         scale=par[:, LN_G + c:LN_G + c + 1]).then_inc(ln_silu, 1)
                    act.wait_ge(ln_silu, l * NC + c + 1)
                    nc.scalar.activation(y_hi[:, c, :], y_conv[:, c, :], ACT.Copy,
                                         scale=par[:, G_CONV + c:G_CONV + c + 1]).then_inc(y_hi_made, 1)
                for c in range(NC):
                    nc.scalar.activation(squares[:, c, :], y_conv[:, c, :], ACT.Square).then_inc(y_squared, 1)
                mix_high(18)
                mix_high(19)
                root(l, "conv", stat_bank["conv"], D_CONV)
                for s in range(20, 24):
                    mix_high(s)
                    for m in (2 * (s - 20), 2 * (s - 20) + 1):
                        act.wait_ge(x_made, l * ND + m + 1)
                        prepare(prep_no(l, 2), m, par, G_FFN2)
                ffn_steps(l, FFN_SLOTS + MIX_SLOTS, FFN_TURNS + MIX_TURNS, "ffn2", last=True)
            root(DEPTH, "ffn1", side_bank, D_MODEL)

        @block.vector
        def _(dve):
            dve.sem_inc(evicted, BANKS)
            dve.sem_inc(rstd_made, 1)
            nc.vector.memset(ones[:], 1.0).then_inc(consts_v, 1)
            dve.wait_ge(consts_p, 1)
            nc.vector.tensor_copy(dist[:], dist_int[:]).then_inc(consts_v, 1)
            dve.wait_ge(consts_v, 2)
            nc.vector.tensor_scalar(dist_neg[:], dist[:], -1.0, None, ALU.mult)
            nc.vector.memset(eps[:], EPS)
            nc.vector.memset(zero[:], 0.0)
            for c in range(NC):
                for kv in range(N_KV_HEADS):
                    nc.vector.memset(q_scale[HEAD_DIM * kv:HEAD_DIM * (kv + 1), c:c + 1],
                                     -1.0 / (math.sqrt(HEAD_DIM) * slope(kv, c)))
            dve.drain().then_inc(small_made, 1)
            dve.wait_ge(small_made, 1)
            nc.vector.tensor_tensor(dist[:], dist[:], dist_neg[:], ALU.max).then_inc(consts_v, 1)

            def split_x(prep, m, gain, gain_at):
                dve.wait_ge(x_hi_made, prep * ND + m + 1)
                nc.vector.scalar_tensor_tensor(chunk(xs_lo, m), chunk(x, m), column(gain, gain_at + m),
                                               chunk(xs_hi, m).bitcast(F32), ALU.mult,
                                               ALU.subtract).then_inc(x_split, 1)

            def recip(l, name, to=rstd):
                dve.wait_ge(std_made, root_no(l, name) + 1)
                nc.vector.reciprocal(to[:], std[:]).then_inc(rstd_made, 1)

            def rstd_ready(l, name):
                dve.wait_ge(rstd_made, root_no(l, name) + 2)

            def tile_summed(l, slot):
                dve.wait_ge(used, slot_no(l, slot) + 1 + RING)

            def scale_tile(b, w, inc=1):
                nc.vector.tensor_tensor(work[:, w, :], bank[b][:], rstd[:], ALU.mult).then_inc(evicted, inc)

            def own(l, turn):
                dve.wait_ge(evicted, turn_no(l, turn) + 1 + BANKS)

            def ffn_steps(l, base, turns, h_base, prep, name, gain_at):
                recip(l, name)
                with dve.Fori(0, NF // 2) as i:
                    rstd_ready(l, name)
                    for j in range(2):
                        f = i * 2 + j
                        h_no = l * 2 * NF + h_base + f
                        for part in (2 * j, 2 * j + 1):
                            tile_summed(l, base + i * 4 + part)
                            scale_tile(part, part)
                        own(l, turns + f * 2 + 1)
                        dve.wait_ge(silu_made, h_no + 1)
                        nc.vector.tensor_tensor(work[:, 2 * j + 1, :], work[:, 2 * j, :], work[:, 2 * j + 1, :],
                                                ALU.mult).then_inc(h_made, 1)
                        dve.wait_ge(h_made, h_no + 1)
                        nc.vector.tensor_scalar(chunk(h_hi, f), work[:, 2 * j + 1, :], 1.0, None,
                                                ALU.mult).then_inc(h_hi_made, 1)
                        dve.wait_ge(h_hi_made, h_no + 1)
                        nc.vector.tensor_tensor(chunk(h_lo, f), work[:, 2 * j + 1, :], chunk(h_hi, f).bitcast(F32),
                                                ALU.subtract).then_inc(h_split, 1)
                with dve.Fori(0, ND // 4) as i:
                    dve.wait_ge(par_landed, l * 16 + 16)
                    for j in range(4):
                        m = i * 4 + j
                        tile_summed(l, base + 2 * NF + m * 4 + 3)
                        nc.vector.scalar_tensor_tensor(chunk(x, m), bank[j][:], 0.5, chunk(x, m), ALU.mult,
                                                       ALU.add).then_inc(evicted, 1)
                        own(l, turns + 2 * NF + m)
                        dve.wait_ge(sq_added, prep * ND + m)
                        nc.vector.tensor_tensor(sq[:], chunk(x, m), chunk(x, m), ALU.mult).then_inc(squared, 1)
                        high_x(m, par, gain_at)
                        split_x(prep, m, par, gain_at)

            def high_x(m, gain, gain_at):
                nc.vector.tensor_scalar(chunk(xs_hi, m), chunk(x, m), column(gain, gain_at + m), None,
                                        ALU.mult).then_inc(x_hi_made, 1)

            dve.wait_ge(gain_landed, 16)
            for m in range(ND):
                if m % 2 == 0:
                    dve.wait_ge(x_landed[m // 2], 16)
                high_x(m, gain0, 0)
                split_x(0, m, gain0, 0)
            for m in range(1, ND):
                dve.wait_ge(squared, m + 1)
                if m > 1:
                    dve.wait_ge(sq_added, m)
                nc.vector.tensor_tensor(sq_sum[:], x_squares[:, 0, :] if m == 1 else sq_sum[:], x_squares[:, m, :],
                                        ALU.add).then_inc(sq_added, 2 if m == 1 else 1)
            with dve.Fori(0, DEPTH) as l:
                ffn_steps(l, 0, 0, 0, prep_no(l, 1), "ffn1", G_MIX)

                def turn(t):
                    return MIX_T + t

                def in_summed(t):
                    tile_summed(l, MIX_S + (t if t < 12 else 13 + 2 * (t - 12)))

                def tile(t, inc=1):
                    in_summed(t)
                    scale_tile(t % BANKS, t % BANKS, inc)

                def out_summed(slot, m):
                    if m % 2:
                        tile_summed(l, MIX_S + slot + m // 2)
                    else:
                        dve.wait_ge(half_used, l * ND + (slot - 16) + m // 2 + 1)

                def gate(c):
                    ta, tg = IN_TILES.index(f"a{c}"), IN_TILES.index(f"g{c}")
                    own(l, turn(ta))
                    dve.wait_ge(sig_made, l * NC + c + 1)
                    nc.vector.tensor_tensor(glu[:, c, CONV_PAD:CONV_PAD + SEQ], work[:, ta % BANKS, :],
                                            work[:, tg % BANKS, :], ALU.mult).then_inc(glu_made, 1)

                def taps(first, count):
                    for n in range(first, first + count):
                        c, t = divmod(n, V_OPS)
                        if t == 0:
                            dve.wait_ge(glu_made, l * NC + c + 1)
                        if t < V_TAPS:
                            h = glu[:, c, t:t + SEQ]
                            w = par[:, CONV_W + c * CONV_WIDTH + t:CONV_W + c * CONV_WIDTH + t + 1]
                        into = y_conv[:, c, :] if t % 2 == 0 else odd_taps[:]
                        if t >= 2 or (c and t == 1):
                            dve.wait_ge(tapped, l * NC * V_OPS + n - (t < V_TAPS))
                        if t == V_TAPS:
                            nc.vector.tensor_tensor(y_conv[:, c, :], y_conv[:, c, :], odd_taps[:],
                                                    ALU.add).then_inc(tapped, 1)
                        elif t == 0:
                            nc.vector.tensor_scalar(into, h, w, par[:, CONV_B + c:CONV_B + c + 1], ALU.mult,
                                                    ALU.add).then_inc(tapped, 1)
                        elif t == 1:
                            nc.vector.tensor_scalar(into, h, w, None, ALU.mult).then_inc(tapped, 1)
                        else:
                            nc.vector.scalar_tensor_tensor(into, h, w, into, ALU.mult, ALU.add).then_inc(tapped, 1)

                def merge(c):
                    dve.wait_ge(tapped, (l * NC + c + 1) * V_OPS)
                    dve.wait_ge(tap_added, (l * NC + c + 1) * P_TAPS)
                    nc.vector.tensor_tensor(y_conv[:, c, :], y_conv[:, c, :], pool_taps[:],
                                            ALU.add).then_inc(taps_merged, 1)

                def low_qk(t, n, hi, lo):
                    own(l, turn(t))
                    dve.wait_ge(qk_hi, l * (NC + 1) + n + 1)
                    nc.vector.tensor_tensor(lo, work[:, t % BANKS, :], hi.bitcast(F32),
                                            ALU.subtract).then_inc(qk_split, 1)

                def bias_scores(g, c, first_tap, n_taps):
                    b, kv = divmod(g, 2)
                    first, n = keys_of(b)
                    at = (first - (b - 1)) * P
                    k = ATT["scores", g, c]
                    if g == 0:
                        dve.wait_ge(consts_p, 5)
                    if g == PROBS - 1:
                        dve.wait_ge(glu_made, l * NC + NC)
                    dve.wait_ge(scored, l * N_UNITS + g * GROUP + c + 1)
                    if g >= PROBS:
                        dve.wait_ge(turned, l * N_UNITS + (g - PROBS) * GROUP + c + 1)
                    taps(first_tap, n_taps)
                    nc.vector.tensor_tensor_reduce(
                        out=probs[g % PROBS][:, c, 0:n * P], in0=att_bank[k % ATT_BANKS][:, 0:n * P],
                        in1=dist[:, at:at + n * P], scale=slope(kv, c),
                        scalar=neg_sink[:, kv * GROUP + c:kv * GROUP + c + 1], op0=ALU.add, op1=ALU.min,
                        accum_out=neg_max[:, g % PROBS, c:c + 1]).then_inc(att_freed, 1)

                def sink_args(g):
                    kv = g % 2
                    dve.wait_ge(att_freed, l * len(ATT) + ATT["scores", g, GROUP - 1] + 1)
                    nc.vector.tensor_tensor(sink_arg[:, g % PROBS, :], neg_max[:, g % PROBS, :],
                                            par[:, SINK + kv * GROUP:SINK + (kv + 1) * GROUP],
                                            ALU.add).then_inc(sink_ready, 1)

                def denominators(g):
                    dve.wait_ge(sink_exped, l * N_GROUPS + g + 1)
                    dve.wait_ge(exped, l * N_UNITS + g * GROUP + GROUP)
                    nc.vector.tensor_tensor(den[:, g % PROBS, :], p_sum[:, g % PROBS, :], sink_exp[:, g % PROBS, :],
                                            ALU.add).then_inc(den_made, 1)
                    dve.wait_ge(den_made, l * N_GROUPS + g + 1)
                    nc.vector.reciprocal(r_den[:, g % PROBS, :], den[:, g % PROBS, :]).then_inc(r_den_made, 1)

                def turned_low(g, c):
                    n = keys_of(g // 2)[1]
                    dve.wait_ge(pt_hi_made, l * N_UNITS + g * GROUP + c + 1)
                    src = att_bank[ATT["turned", g, c] % ATT_BANKS][:, 0:n * P].rearrange("p (k q) -> p k q", q=P)
                    nc.vector.tensor_tensor(pt_lo[:, g % 2, 0:n, c, :], src, pt_hi[:, g % 2, 0:n, c, :].bitcast(F32),
                                            ALU.subtract).then_inc(att_freed, 1)

                def evict_o(g):
                    b, kv = divmod(g, 2)
                    rows = slice(HEAD_DIM * kv, HEAD_DIM * (kv + 1))
                    dve.wait_ge(o_made, l * N_GROUPS + g + 1)
                    nc.vector.tensor_copy(y_attn[rows, :, b * P:(b + 1) * P],
                                          side_bank[rows, :].rearrange("p (c q) -> p c q", q=P)).then_inc(o_evicted, 1)

                nc.vector.memset(glu[:, :, 0:CONV_PAD], 0.0).then_inc(padded, 1)
                nc.vector.memset(glu[:, :, CONV_PAD + SEQ:], 0.0).then_inc(padded, 1)
                nc.vector.tensor_scalar(neg_sink[:], par[:, SINK:SINK + N_Q_HEADS], -1.0, None,
                                        ALU.mult).then_inc(neg_sink_made, 1)
                dve.wait_ge(padded, l * 2 + 2)
                dve.wait_ge(neg_sink_made, l + 1)
                recip(l, "mix")
                rstd_ready(l, "mix")
                tile(0)
                tile(1)
                gate(0)
                done = 0
                for t in range(2, 12):
                    name = IN_TILES[t]
                    if name[0] == "q":
                        c = int(name[1])
                        in_summed(t)
                        nc.vector.scalar_tensor_tensor(work[:, t % BANKS, :], bank[t % BANKS][:], q_scale[:, c:c + 1],
                                                       rstd[:], ALU.mult, ALU.mult).then_inc(evicted, 1)
                    else:
                        tile(t)
                    taps(done, V_SPREAD[t - 2])
                    done += V_SPREAD[t - 2]
                    if name[0] == "g":
                        gate(int(name[1]))
                    elif name == "k":
                        low_qk(t, 0, k_hi[:], k_lo[:])
                    elif name == "v":
                        merge(0)
                    elif name[0] == "q":
                        low_qk(t, 1 + c, q_hi[:, c, :], q_lo[:, c, :])
                        if c == 0:
                            dve.wait_ge(v_hi_made, l + 1)
                            nc.vector.tensor_tensor(v_lo[:].rearrange("p b d -> p (b d)"), side_bank[:],
                                                    v_hi[:].rearrange("p b d -> p (b d)").bitcast(F32),
                                                    ALU.subtract).then_inc(v_split, 1)
                tile(12)
                for c in range(GROUP):
                    bias_scores(0, c, done, 1)
                    done += 1
                sink_args(0)
                for c in range(GROUP):
                    bias_scores(1, c, done, 1)
                    done += 1
                    if c == 0:
                        denominators(0)
                sink_args(1)
                tile(13, inc=3)
                gate(3)
                for g in range(N_GROUPS):
                    for c in range(GROUP):
                        turned_low(g, c)
                        if g + AHEAD < N_GROUPS:
                            bias_scores(g + AHEAD, c, done, 1)
                            done += 1
                        if c == 1 and g + 1 < N_GROUPS:
                            denominators(g + 1)
                        if c == 3 and g:
                            evict_o(g - 1)
                        for of, at in enumerate(MERGED_AT, 1):
                            if (g, c) == at:
                                merge(of)
                    if g + AHEAD < N_GROUPS:
                        sink_args(g + AHEAD)
                evict_o(N_GROUPS - 1)
                assert done == NC * V_OPS, done

                for c in range(NC):
                    dve.wait_ge(y_hi_made, l * 2 * NC + c + 1)
                    nc.vector.scalar_tensor_tensor(xs_lo[:, c, :], y_attn[:, c, :], par[:, G_ATTN + c:G_ATTN + c + 1],
                                                   xs_hi[:, c, :].bitcast(F32), ALU.mult,
                                                   ALU.subtract).then_inc(y_split, 1)
                recip(l, "attn")
                rstd_ready(l, "attn")

                def out_a(m):
                    if m >= BANKS:
                        dve.wait_ge(x_half, l * ND + m - BANKS + 1)
                    out_summed(16, m)
                    scale_tile(m % BANKS, m % BANKS)

                for c in range(NC):
                    if c == 0:
                        dve.wait_ge(stat_made, stat_no(l, "mean") + 1)
                    nc.vector.scalar_tensor_tensor(y_conv[:, c, :], stat_bank["mean"][:], -1.0 / D_CONV,
                                                   y_conv[:, c, :], ALU.mult, ALU.add).then_inc(centred, 1)
                for m in range(4):
                    out_a(m)
                recip(l, "var", ln_rstd)
                rstd_ready(l, "var")
                for c in range(NC):
                    dve.wait_ge(y_squared, l * 3 * NC + NC + c + 1)
                    nc.vector.tensor_tensor(y_conv[:, c, :], y_conv[:, c, :], ln_rstd[:],
                                            ALU.mult).then_inc(ln_scaled, 1)
                for m in range(4, ND):
                    out_a(m)
                for c in range(NC):
                    dve.wait_ge(y_hi_made, l * 2 * NC + NC + c + 1)
                    nc.vector.scalar_tensor_tensor(y_lo[:, c, :], y_conv[:, c, :],
                                                   par[:, G_CONV + c:G_CONV + c + 1],
                                                   y_hi[:, c, :].bitcast(F32), ALU.mult,
                                                   ALU.subtract).then_inc(y_split, 1)
                own(l, turn(OUT_A_TURN + ND - 1))
                recip(l, "conv")
                rstd_ready(l, "conv")
                dve.wait_ge(x_half, l * ND + ND)
                for m in range(ND):
                    out_summed(20, m)
                    scale_tile(m % BANKS, m % BANKS)
                    own(l, turn(OUT_C_TURN + m))
                    nc.vector.tensor_tensor(x[:, m, :], x[:, m, :], work[:, m % BANKS, :],
                                            ALU.add).then_inc(x_made, 1)
                    dve.wait_ge(x_made, l * ND + m + 1)
                    split_x(prep_no(l, 2), m, par, G_FFN2)
                ffn_steps(l, FFN_SLOTS + MIX_SLOTS, FFN_TURNS + MIX_TURNS, NF, prep_no(l, 3), "ffn2", G_NEXT)

            recip(DEPTH, "ffn1")
            rstd_ready(DEPTH, "ffn1")
            for m in range(ND):
                nc.vector.scalar_tensor_tensor(result[:, m, :], x[:, m, :], par[:, G_NEXT + m:G_NEXT + m + 1],
                                               rstd[:], ALU.mult, ALU.mult).then_inc(result_made, 1)

        @block.tensor
        def _(pe):
            pe.sem_inc(used, RING)

            def triple(to, wh, wl, mh, ml, first, last):
                nc.tensor.matmul(to, wh, mh, start=first, stop=False)
                nc.tensor.matmul(to, wh, ml, start=False, stop=False)
                return nc.tensor.matmul(to, wl, mh, start=False, stop=last)

            def weights(r, i):
                at = slice(i * P, (i + 1) * P)
                return w_hi[:, r, at], w_lo[:, r, at]

            def take(l, n):
                pe.wait_ge(split, slot_no(l, n) + 1 + RING)

            def open_bank(l, turn):
                pe.wait_ge(evicted, turn_no(l, turn) + 1)

            def statistic(l, name):
                pe.wait_ge(sq_added, l * 3 * ND + {"ffn1": ND, "mix": 2 * ND, "ffn2": 3 * ND}[name])
                nc.tensor.matmul(side_bank[:], ones[:], sq_sum[:], start=True, stop=True).then_inc(stat_made, 1)

            def statistic_of(l, to, ready, base, chunks):
                for c in range(NC):
                    pe.wait_ge(ready, base + (c + 1))
                    last = nc.tensor.matmul(to[:], ones[:], chunks[:, c, :], start=c == 0, stop=c == NC - 1)
                last.then_inc(stat_made, 1)

            def model_tile(l, n, r, turn, b, prep=None, part=(0, ND)):
                first, end = part
                take(l, n)
                if first == 0:
                    open_bank(l, turn)
                for k in range(first, end):
                    if prep is not None:
                        pe.wait_ge(x_split, prep * ND + k + 1)
                    last = triple(bank[b][:], *weights(r, k - first), xs_hi[:, k, :], xs_lo[:, k, :], k == 0,
                                  k == ND - 1)
                last.then_inc(used, 1)

            def ffn_steps(l, base, turns, h_base, prep, name):
                for j in range(4):
                    model_tile(l, base + j, j, turns + j, j, prep if j == 0 else None)
                    if j == 0:
                        statistic(l, name)
                with pe.Fori(1, NF // 2) as i:
                    for j in range(4):
                        model_tile(l, base + i * 4 + j, j, turns + i * 4 + j, j)
                with pe.Fori(0, ND // 4) as i:
                    for j in range(4):
                        turn = turns + 2 * NF + i * 4 + j
                        open_bank(l, turn)
                        f = 0
                        for s, count in enumerate(DOWN):
                            take(l, base + 2 * NF + (i * 4 + j) * 4 + s)
                            pe.wait_ge(h_split, l * 2 * NF + h_base + f + count)
                            for k in range(count):
                                last = triple(bank[j][:], *weights(s, k), h_hi[:, f, :], h_lo[:, f, :], f == 0,
                                              f == NF - 1)
                                f += 1
                            last.then_inc(used, 1)

            pe.wait_ge(consts_v, 1)
            pe.wait_ge(consts_p, 3)
            with pe.Fori(0, DEPTH) as l:
                ffn_steps(l, 0, 0, 0, prep_no(l, 0), "ffn1")

                def in_tile(t):
                    model_tile(l, MIX_S + t, t % RING, MIX_T + t, t % BANKS, prep_no(l, 1) if t == 0 else None)

                def half_tile(t, half):
                    s = 12 + 2 * (t - 12) + half
                    model_tile(l, MIX_S + s, s % RING, MIX_T + t, t % BANKS, part=(4 * half, 4 * half + 4))

                def scores(g, c):
                    b, kv = divmod(g, 2)
                    first, n = keys_of(b)
                    k = ATT["scores", g, c]
                    rows = slice(HEAD_DIM * kv, HEAD_DIM * (kv + 1))
                    q, keys = slice(b * P, (b + 1) * P), slice(first * P, (first + n) * P)
                    to = att_bank[k % ATT_BANKS][:, 0:n * P]
                    if k >= ATT_BANKS:
                        pe.wait_ge(att_freed, l * len(ATT) + k - ATT_BANKS + 1)
                    elif k >= 3:
                        pe.wait_ge(evicted, turn_no(l, MIX_T + 12) + 1 + BANKS)
                    nc.tensor.matmul(to, q_hi[rows, c, q], k_hi[rows, keys], start=True, stop=False)
                    nc.tensor.matmul(to, q_hi[rows, c, q], k_lo[rows, keys], start=False, stop=False)
                    nc.tensor.matmul(to, q_lo[rows, c, q], k_hi[rows, keys], start=False,
                                     stop=True).then_inc(scored, 1)

                def turn_weights(g, c):
                    n = keys_of(g // 2)[1]
                    k = ATT["turned", g, c]
                    half = GROUP // 2
                    pe.wait_ge(normed_a if c < half else normed_p, (l * N_GROUPS + g) * half + c % half + 1)
                    pe.wait_ge(att_freed, l * len(ATT) + k - ATT_BANKS + 1)
                    for i in range(n):
                        last = nc.tensor.transpose(att_bank[k % ATT_BANKS][:, i * P:(i + 1) * P],
                                                   probs[g % PROBS][:, c, i * P:(i + 1) * P], ident[:])
                    last.then_inc(turned, 1)

                def weigh_values(g):
                    first, n = keys_of(g // 2)
                    pe.wait_ge(att_freed, l * len(ATT) + ATT["turned", g, GROUP - 1] + 1)
                    if g:
                        pe.wait_ge(o_evicted, l * N_GROUPS + g)
                    for i in range(n):
                        mh = pt_hi[:, g % 2, i, :, :].rearrange("p c q -> p (c q)")
                        ml = pt_lo[:, g % 2, i, :, :].rearrange("p c q -> p (c q)")
                        last = triple(side_bank[:], v_hi[:, first + i, :], v_lo[:, first + i, :], mh, ml, i == 0,
                                      i == n - 1)
                    last.then_inc(o_made, 1)

                def out_tiles(first_slot, first_turn, hi, lo, done, between):
                    for m in range(ND):
                        s = first_slot + m // 2
                        if m % 2 == 0:
                            take(l, MIX_S + s)
                        open_bank(l, MIX_T + first_turn + m)
                        for c in range(NC):
                            if m == 0:
                                pe.wait_ge(y_split, l * 2 * NC + done + c + 1)
                            last = triple(bank[m % BANKS][:], *weights(s % RING, 4 * (m % 2) + c),
                                          hi[:, c, :], lo[:, c, :], c == 0, c == NC - 1)
                        last.then_inc(used if m % 2 else half_used, 1)
                        if m in between:
                            between[m]()

                in_tile(0)
                statistic(l, "mix")
                for t in range(1, 9):
                    in_tile(t)
                pe.wait_ge(evicted, turn_no(l, MIX_T + IN_TILES.index("v")) + 1 + BANKS)
                pe.wait_ge(std_made, root_no(l, "mix") + 1)
                for b in range(NB):
                    last = nc.tensor.transpose(side_bank[:, b * P:(b + 1) * P],
                                               work[:, IN_TILES.index("v") % BANKS, b * P:(b + 1) * P], ident[:])
                last.then_inc(v_turned, 1)
                for t in range(9, 12):
                    in_tile(t)
                half_tile(12, 0)
                half_tile(12, 1)
                pe.wait_ge(qk_split, l * (NC + 1) + NC + 1)
                ahead = [(g, c) for g in range(AHEAD) for c in range(GROUP)]
                for g, c in ahead[:3]:
                    scores(g, c)
                half_tile(13, 0)
                for g, c in ahead[3:6]:
                    scores(g, c)
                half_tile(13, 1)
                for g, c in ahead[6:]:
                    scores(g, c)
                pe.wait_ge(v_split, l + 1)
                for g in range(N_GROUPS):
                    for c in range(GROUP):
                        turn_weights(g, c)
                        if g + AHEAD < N_GROUPS:
                            scores(g + AHEAD, c)
                        if c == 2 and g:
                            weigh_values(g - 1)
                weigh_values(N_GROUPS - 1)

                def attn_stat():
                    statistic_of(l, stat_bank["attn"], y_squared, l * 3 * NC, squares)

                def mean_stat():
                    statistic_of(l, stat_bank["mean"], taps_merged, l * NC, y_conv)

                def var_stat():
                    statistic_of(l, stat_bank["var"], y_squared, l * 3 * NC + NC, squares)

                out_tiles(16, OUT_A_TURN, xs_hi, xs_lo, 0, {0: attn_stat, 1: mean_stat, 4: var_stat})

                def conv_stat():
                    statistic_of(l, stat_bank["conv"], y_squared, l * 3 * NC + 2 * NC, squares)

                out_tiles(20, OUT_C_TURN, y_hi, y_lo, NC, {0: conv_stat})
                ffn_steps(l, FFN_SLOTS + MIX_SLOTS, FFN_TURNS + MIX_TURNS, NF, prep_no(l, 2), "ffn2")
            pe.wait_ge(sq_added, (DEPTH * 3 + 1) * ND)
            nc.tensor.matmul(side_bank[:], ones[:], sq_sum[:], start=True, stop=True).then_inc(stat_made, 1)


def by_partition(v):
    return v.reshape(v.shape[0], -1, P).transpose(0, 2, 1)


def tiles_of(w, n_out):
    *lead, k, n = w.shape
    w = w.reshape(*lead, k // P, P, n // n_out, n_out)
    d = len(lead)
    w = w.transpose(*range(d), d + 2, d + 1, d, d + 3)
    return w.reshape(*lead, n // n_out, P, k // P * n_out)


def heads_paired(v, axis):
    shape = v.shape
    v = v.reshape(*shape[:axis], N_KV_HEADS, GROUP, HEAD_DIM, *shape[axis + 1:])
    return v.swapaxes(axis, axis + 1).reshape(shape)


def kernel(**inputs):
    import concourse.bacc as bacc
    from concourse.bass_utils import run_bass_kernel_spmd

    a = {k: np.asarray(v) for k, v in inputs.items()}
    next_norm = np.concatenate([a["ffn1_norm"][1:], a["final_norm"][None]], axis=0)
    conv_w = a["conv_w"].transpose(0, 2, 1).reshape(DEPTH, NC, P, CONV_WIDTH).transpose(0, 2, 1, 3)
    params = np.concatenate([
        by_partition(a["mix_norm"]), by_partition(a["ffn2_norm"]), by_partition(next_norm),
        conv_w.reshape(DEPTH, P, NC * CONV_WIDTH), by_partition(a["conv_b"]), by_partition(a["conv_ln_g"]),
        by_partition(a["conv_ln_b"]), by_partition(a["out_norm_conv"]),
        by_partition(heads_paired(a["out_norm_attn"], 1)),
        np.broadcast_to(a["attn_sink"][:, None, :], (DEPTH, P, N_Q_HEADS)),
    ], axis=2)

    def gate_up(ffn):
        both = np.stack([tiles_of(a[f"{ffn}_w_gate"], P), tiles_of(a[f"{ffn}_w_up"], P)], axis=2)
        return both.reshape(DEPTH, 2 * NF, P, 8 * P)

    w_in = a["w_in"]
    conv_in, q_in, kv_in = w_in[..., :2 * D_CONV], w_in[..., 2 * D_CONV:3 * D_CONV], w_in[..., 3 * D_CONV:]
    in_tiles = tiles_of(np.concatenate([conv_in, heads_paired(q_in, 2), kv_in], axis=2), P)
    order = {"a": 0, "g": NC, "q": 2 * NC, "k": 3 * NC, "v": 3 * NC + 1}
    in_order = [order[t[0]] + int(t[1:] or 0) for t in IN_TILES]
    w_out = a["w_out"]
    out_a = tiles_of(heads_paired(w_out[:, D_CONV:], 1), P)
    out_c = tiles_of(w_out[:, :D_CONV], P)
    pair = [t.reshape(DEPTH, ND // 2, 2, P, 4 * P).transpose(0, 1, 3, 2, 4).reshape(DEPTH, ND // 2, P, 8 * P)
            for t in (out_a, out_c)]
    arrays = {
        "xT": a["x"].reshape(SEQ, D_MODEL).T,
        "first_gain": by_partition(a["ffn1_norm"])[0],
        "params": params,
        "w_gu": np.stack([gate_up("ffn1"), gate_up("ffn2")], axis=1),
        "w_down": np.stack([tiles_of(a["ffn1_w_down"], P), tiles_of(a["ffn2_w_down"], P)], axis=1),
        "w_in": in_tiles[:, in_order],
        "w_out": np.concatenate(pair, axis=1),
    }
    arrays = {k: np.ascontiguousarray(v) for k, v in arrays.items()}
    nc = bacc.Bacc("TRN2", target_bir_lowering=False, num_devices=1)
    args = [nc.dram_tensor(k, v.shape, mybir.dt.from_np(v.dtype), kind="ExternalInput").ap()
            for k, v in arrays.items()]
    out = nc.dram_tensor("out", (D_MODEL, SEQ), F32, kind="ExternalOutput").ap()
    encoder(nc, *args, out)
    r = run_bass_kernel_spmd(nc, [arrays], core_ids=[0])
    return np.ascontiguousarray(r.results[0]["out"].T).reshape(1, SEQ, D_MODEL)
```

```python
import math
from contextlib import ExitStack

import numpy as np

import concourse.bass as bass
from concourse import mybir

P = 128
D_MODEL, SEQ, DEPTH, D_FF = 1024, 512, 2, 2816
D_CONV, CONV_WIDTH, HEAD_DIM = 512, 31, 64
N_Q_HEADS, N_KV_HEADS = 8, 2
GROUP = N_Q_HEADS // N_KV_HEADS
CONV_PAD = CONV_WIDTH // 2
EPS = 1e-6
MASKED = 1e30

ND = D_MODEL // P
NF = D_FF // P
NC = D_CONV // P
NB = SEQ // P
RING = 4
BANKS = 4
DOWN = (6, 6, 5, 5)
assert sum(DOWN) == NF

IN_TILES = ["a0", "g0", "a1", "g1", "a2", "g2", "k", "v", "q0", "q1", "q2", "q3", "a3", "g3"]
IN_SLOTS = [(t,) for t in range(12)] + [(12, 0), (12, 1), (13, 0), (13, 1)]

FFN_SLOTS, MIX_SLOTS = 2 * NF + 4 * ND, 24
LAYER_SLOTS = 2 * FFN_SLOTS + MIX_SLOTS
FFN_TURNS, MIX_TURNS = 2 * NF + ND, 32
LAYER_TURNS = 2 * FFN_TURNS + MIX_TURNS
OUT_A_TURN, OUT_C_TURN = 16, 24
assert LAYER_SLOTS % RING == 0 and LAYER_TURNS % BANKS == 0

STATS = ["ffn1", "mix", "mean", "var", "attn", "conv", "ffn2"]
ROOTS = [s for s in STATS if s != "mean"]
BY_TOKEN = ["var", "attn"]

G_MIX, G_FFN2, G_NEXT = 0, 8, 16
CONV_W = 24
CONV_B = CONV_W + NC * CONV_WIDTH
LN_G, LN_B, G_CONV, G_ATTN = CONV_B + 4, CONV_B + 8, CONV_B + 12, CONV_B + 16
SINK = CONV_B + 20
N_PAR = SINK + N_Q_HEADS

ALU = mybir.AluOpType
ACT = mybir.ActivationFunctionType
F32 = mybir.dt.float32
F32R = mybir.dt.float32r
I32 = mybir.dt.int32


def keys_of(b):
    first = max(0, b - 1)
    return first, min(NB, b + 2) - first


def slope(kv, c):
    return 2.0 ** (-8.0 * (kv * GROUP + c + 1) / N_Q_HEADS)


FINAL_SPLIT = 5
FINAL_ORDER = list(range(FINAL_SPLIT, ND)) + list(range(FINAL_SPLIT))
AHEAD = 2
PROBS = AHEAD + 1


def attention_turns():
    turns = [("scores", g, c) for g in range(AHEAD) for c in range(GROUP)]
    for g in range(2 * NB):
        for c in range(GROUP):
            turns.append(("turned", g, c))
            if g + AHEAD < 2 * NB:
                turns.append(("scores", g + AHEAD, c))
    return {use: n for n, use in enumerate(turns)}


ATT = attention_turns()
ATT_BANKS = 6
N_GROUPS = 2 * NB
N_UNITS = N_GROUPS * GROUP
V_TAPS = 20
P_TAPS = CONV_WIDTH - V_TAPS
V_OPS = V_TAPS + 1
V_SPREAD = [5] * 8 + [6] * 2
P_SPREAD = [2] * 10 + [2, 4, 4, 4, 3, 3, 3, 1]
PRODUCT_HEADS = {4: (0, 1, 2, 3), 3: (0, 1, 3), 1: (0,), 0: ()}
MERGED_AT = {(3, 0): 2, (6, 2): 3}
assert sum(V_SPREAD) + 4 * N_GROUPS == NC * V_OPS and sum(P_SPREAD) == NC * P_TAPS


def encoder(nc, xT, first_gain, params, w_gu, w_down, w_in, w_out, out):
    with ExitStack() as ctx:
        def sb(name, shape, dt=F32, stack=ctx):
            return stack.enter_context(nc.sbuf_tensor(name, shape, dt))

        def sem(name):
            return ctx.enter_context(nc.semaphore(name))

        x = sb("x", [P, ND, SEQ])
        xs_hi = sb("xs_hi", [P, ND, SEQ], F32R)
        xs_lo = sb("xs_lo", [P, ND, SEQ], F32R)
        stage = sb("stage", [P, RING, 8 * P])
        w_hi = sb("w_hi", [P, RING, 8 * P], F32R)
        w_lo = sb("w_lo", [P, RING, 8 * P], F32R)
        work = sb("work", [P, BANKS, SEQ])
        sq = sb("sq", [P, SEQ])
        sq_sum = sb("sq_sum", [P, SEQ])
        zero = sb("zero", [P, 1])
        pool_taps = sb("pool_taps", [P, SEQ])
        std = sb("std", [P, SEQ])
        std_token = sb("std_token", [P, NB])
        rstd_token = sb("rstd_token", [P, 2, NB])
        rstd = sb("rstd", [P, SEQ])
        dist = sb("dist", [P, 3 * P])
        ident = sb("ident", [P, P])
        diag = sb("diag", [P, GROUP, P])
        ones = sb("ones", [P, P])
        q_scale = sb("q_scale", [P, NC])
        eps = sb("eps", [P, 1])
        gain0 = sb("gain0", [P, ND])
        par = sb("par", [P, N_PAR])
        neg_sink = sb("neg_sink", [P, N_Q_HEADS])
        neg_max = sb("neg_max", [P, PROBS, GROUP])
        p_sum = sb("p_sum", [P, PROBS, GROUP])
        sink_arg = sb("sink_arg", [P, PROBS, GROUP])
        sink_exp = sb("sink_exp", [P, PROBS, GROUP])
        den = sb("den", [P, PROBS, GROUP])
        r_den = sb("r_den", [P, PROBS, GROUP])

        with ExitStack() as region:
            h_hi = sb("h_hi", [P, NF, SEQ], F32R, region)
            h_lo = sb("h_lo", [P, NF, SEQ], F32R, region)
        with ExitStack() as region:
            prob = sb("prob", [P, 2, GROUP, 3 * P], F32, region)
            pt_hi = sb("pt_hi", [P, 2, 3, GROUP, P], F32R, region)
            pt_lo = sb("pt_lo", [P, 2, 3, GROUP, P], F32R, region)
            glu = sb("glu", [P, NC, SEQ + 2 * CONV_PAD], F32, region)
            y_conv = sb("y_conv", [P, NC, SEQ], F32, region)
            odd_taps = sb("odd_taps", [P, SEQ], F32, region)
            q_hi = sb("q_hi", [P, NC, SEQ], F32R, region)
            q_lo = sb("q_lo", [P, NC, SEQ], F32R, region)
            k_hi = sb("k_hi", [P, SEQ], F32R, region)
            k_lo = sb("k_lo", [P, SEQ], F32R, region)
            v_hi = sb("v_hi", [P, NB, P], F32R, region)
            v_lo = sb("v_lo", [P, NB, P], F32R, region)
            y_attn = sb("y_attn", [P, NC, SEQ], F32, region)
        probs = [prob[:, i] for i in range(2)]
        probs.append(work[:].rearrange("p m n -> p (m n)")[:, 0:GROUP * 3 * P]
                     .rearrange("p (c n) -> p c n", c=GROUP))
        channel_squares = work
        squares = prob[:].rearrange("p a c n -> p (a c n)")[:, 0:NC * SEQ].rearrange("p (c n) -> p c n", c=NC)
        product = [sq, sq_sum, std]
        x_square = [sq, pool_taps]
        channel_sum = rstd
        y_hi, y_lo = q_hi, q_lo
        with ExitStack() as region:
            result = sb("result", [P, ND, SEQ], F32, region)
            dist_int = sb("dist_int", [P, 3 * P], I32, region)
            dist_neg = sb("dist_neg", [P, 3 * P], F32, region)
        x_squares = result

        bank = [ctx.enter_context(nc.psum_tensor(f"bank{i}", [P, SEQ], F32)) for i in range(8)]
        att_bank, side_bank = bank[4:7] + [bank[0], bank[2], bank[3]], bank[7]

        landed = [sem(f"landed{i}") for i in range(RING)]
        gain_landed = sem("gain_landed")
        x_landed = [sem(f"x_landed{i}") for i in range(4)]
        par_landed = sem("par_landed")
        hi_made = sem("hi_made")
        split = sem("split")
        used = sem("used")
        half_used = sem("half_used")
        evicted = sem("evicted")
        silu_made = sem("silu_made")
        h_made = sem("h_made")
        h_hi_made = sem("h_hi_made")
        h_split = sem("h_split")
        x_made = sem("x_made")
        x_half = sem("x_half")
        x_hi_made = sem("x_hi_made")
        x_split = sem("x_split")
        squares_added = sem("squares_added")
        result_added = sem("result_added")
        channels_added = sem("channels_added")
        spread = sem("spread")
        rstd_copied = sem("rstd_copied")
        squared = sem("squared")
        sq_added = sem("sq_added")
        stat_made = sem("stat_made")
        std_made = sem("std_made")
        rstd_made = sem("rstd_made")
        consts_v = sem("consts_v")
        consts_p = sem("consts_p")
        small_made = sem("small_made")
        padded = sem("padded")
        tanh_made = sem("tanh_made")
        glu_made = sem("glu_made")
        tapped = sem("tapped")
        tap_product = sem("tap_product")
        tap_added = sem("tap_added")
        taps_merged = sem("taps_merged")
        qk_hi = sem("qk_hi")
        qk_split = sem("qk_split")
        v_turned = sem("v_turned")
        v_hi_made = sem("v_hi_made")
        v_split = sem("v_split")
        scored = sem("scored")
        att_freed = sem("att_freed")
        exped = sem("exped")
        sink_ready = sem("sink_ready")
        sink_exped = sem("sink_exped")
        den_made = sem("den_made")
        r_den_made = sem("r_den_made")
        diag_made = sem("diag_made")
        turned = sem("turned")
        pt_hi_made = sem("pt_hi_made")
        o_made = sem("o_made")
        o_evicted = sem("o_evicted")
        y_hi_made = sem("y_hi_made")
        y_split = sem("y_split")
        y_squared = sem("y_squared")
        centred = sem("centred")
        ln_scaled = sem("ln_scaled")
        ln_silu = sem("ln_silu")
        neg_sink_made = sem("neg_sink_made")
        gained = sem("gained")
        result_v = sem("result_v")
        result_p = sem("result_p")
        stored = sem("stored")

        def slot_no(l, n):
            return l * LAYER_SLOTS + n

        def turn_no(l, n):
            return l * LAYER_TURNS + n

        def stat_no(l, name):
            return l * len(STATS) + STATS.index(name)

        def root_no(l, name):
            return l * len(ROOTS) + ROOTS.index(name)

        def spread_no(l, name):
            return l * len(BY_TOKEN) + BY_TOKEN.index(name)

        def prep_no(l, which):
            return l * 3 + which

        def chunk(t, m):
            return t[:, m, :] if isinstance(m, int) else t[:, bass.ds(m, 1), :].rearrange("p o n -> p (o n)")

        def column(t, m):
            return t[:, m:m + 1] if isinstance(m, int) else t[:, bass.ds(m, 1)]

        FFNS = [(0, 0, 0, 0, "ffn1"), (FFN_SLOTS + MIX_SLOTS, FFN_TURNS + MIX_TURNS, NF, 2, "ffn2")]
        MIX_S, MIX_T = FFN_SLOTS, FFN_TURNS
        stat_bank = {"ffn1": side_bank, "mix": side_bank, "ffn2": side_bank, "attn": side_bank, "mean": att_bank[0], "var": att_bank[1], "conv": att_bank[2]}

        block = ctx.enter_context(nc.Block())

        @block.sync
        def _(sp):
            def load(l, n, r, src, width):
                sp.wait_ge(split, slot_no(l, n) + 1)
                sp.dma_start(stage[:, r, 0:width], src).then_inc(landed[r], 16)

            def ffn_loads(l, which, base):
                with sp.Fori(0, 2 * NF // RING) as i:
                    for j in range(RING):
                        src = w_gu[bass.ds(l, 1), which, bass.ds(i * RING + j, 1)]
                        load(l, base + i * RING + j, j, src.rearrange("o t p n -> p (o t n)"), 8 * P)
                if which == 0:
                    sp.wait_ge(x_split, prep_no(l, 0) * ND + ND)
                    sp.dma_start(par[:], params[bass.ds(l, 1)].rearrange("o p n -> p (o n)")).then_inc(par_landed, 16)
                with sp.Fori(0, ND) as m:
                    at = 0
                    for j, count in enumerate(DOWN):
                        src = w_down[bass.ds(l, 1), which, bass.ds(m, 1), :, at:at + count * P]
                        load(l, base + 2 * NF + m * 4 + j, j, src.rearrange("o t p n -> p (o t n)"), count * P)
                        at += count * P

            with sp.Fori(0, DEPTH) as l:
                ffn_loads(l, 0, 0)
                for s, (t, *half) in enumerate(IN_SLOTS):
                    width = 4 * P if half else 8 * P
                    start = 4 * P * half[0] if half else 0
                    src = w_in[bass.ds(l, 1), t, :, start:start + width].rearrange("o p n -> p (o n)")
                    load(l, MIX_S + s, s % RING, src, width)
                for s in range(8):
                    src = w_out[bass.ds(l, 1), s].rearrange("o p n -> p (o n)")
                    load(l, MIX_S + 16 + s, s % RING, src, 8 * P)
                ffn_loads(l, 1, FFN_SLOTS + MIX_SLOTS)

            out_v = out.rearrange("(k p) n -> p k n", p=P)
            for m in [0, 1, FINAL_SPLIT, 2, 3, FINAL_SPLIT + 1, 4, FINAL_SPLIT + 2]:
                if m < FINAL_SPLIT:
                    sp.wait_ge(result_v, m + 1)
                else:
                    sp.wait_ge(result_p, m - FINAL_SPLIT + 1)
                sp.dma_start(out_v[:, m, :], result[:, m, :]).then_inc(stored, 16)
            sp.wait_ge(stored, 16 * ND)

        @block.gpsimd
        def _(pool):
            pool.sem_inc(split, 1)
            nc.gpsimd.iota(dist_int[:], pattern=[[-1, 3 * P]], base=P, channel_multiplier=1).then_inc(consts_p, 1)
            nc.gpsimd.memset(ident[:], 0.0).then_inc(consts_p, 1)
            pool.wait_ge(consts_p, 2)
            nc.gpsimd.affine_select(out=ident[:], in_=ident[:], compare_op=ALU.not_equal, fill=1.0, base=0,
                                    pattern=[[-1, P]], channel_multiplier=1).then_inc(consts_p, 1)
            pool.wait_ge(consts_v, 3)
            nc.gpsimd.affine_select(out=dist[:], in_=dist[:], compare_op=ALU.is_ge, fill=MASKED, base=0,
                                    pattern=[[1, 3 * P]], channel_multiplier=-1).then_inc(consts_p, 1)
            pool.wait_ge(consts_p, 4)
            nc.gpsimd.affine_select(out=dist[:], in_=dist[:], compare_op=ALU.is_ge, fill=MASKED, base=2 * P,
                                    pattern=[[-1, 3 * P]], channel_multiplier=1).then_inc(consts_p, 1)

            def low(l, n, r):
                pool.wait_ge(hi_made, slot_no(l, n) + 1)
                nc.gpsimd.tensor_tensor(w_lo[:, r, :], stage[:, r, :], w_hi[:, r, :].bitcast(F32),
                                        ALU.subtract).then_inc(split, 1)

            def add_square(prep, m, first=False, of=sq):
                pool.wait_ge(squared, prep * ND + m + 1)
                if not first:
                    pool.wait_ge(sq_added, prep * ND + m)
                start = zero[:, 0:1].to_broadcast([P, SEQ])
                nc.gpsimd.tensor_tensor(sq_sum[:], start if first else sq_sum[:], of[:],
                                        ALU.add).then_inc(sq_added, 1)

            def ffn_steps(l, base, next_prep, last):
                with pool.Fori(0, NF // 2) as i:
                    for j in range(4):
                        low(l, base + i * 4 + j + RING, j)
                at = base + 2 * NF
                for j in range(4):
                    low(l, at + RING + j, j)
                add_square(next_prep, 0, first=True)
                with pool.Fori(1, ND - 1) as m:
                    for j in range(4):
                        low(l, at + m * 4 + RING + j, j)
                    add_square(next_prep, m)
                if not last:
                    for j in range(4):
                        low(l, at + ND * 4 + j, j)
                    add_square(next_prep, ND - 1)

            pool.wait_ge(small_made, 1)
            pool.wait_ge(x_landed[0], 16)
            pool.sem_inc(split, RING - 1)
            with pool.Fori(0, DEPTH) as l:
                for j in range(RING):
                    low(l, j, j)
                add_square(prep_no(l, 0), ND - 1)
                ffn_steps(l, 0, prep_no(l, 1), last=False)

                def mix_low(s):
                    low(l, MIX_S + s + RING, s % RING)

                def add_products(first, count):
                    for n in range(first, first + count):
                        c, t = divmod(n, P_TAPS)
                        if n:
                            pool.wait_ge(tap_added, l * NC * P_TAPS + n)
                        if t == 0 and c:
                            pool.wait_ge(taps_merged, l * NC + c)
                        pool.wait_ge(tap_product, l * NC * P_TAPS + n + 1)
                        start = zero[:, 0:1].to_broadcast([P, SEQ])
                        nc.gpsimd.tensor_tensor(pool_taps[:], start if t == 0 else pool_taps[:], product[n % 3][:],
                                                ALU.add).then_inc(tap_added, 1)

                def diagonals(g):
                    pool.wait_ge(r_den_made, l * N_GROUPS + g + 1)
                    for c in range(GROUP):
                        if g:
                            pool.wait_ge(turned, l * N_UNITS + (g - 1) * GROUP + c + 1)
                        nc.gpsimd.tensor_tensor(diag[:, c, :], ident[:],
                                                r_den[:, g % PROBS, c:c + 1].to_broadcast([P, P]),
                                                ALU.mult).then_inc(diag_made, 1)

                def add_channel(c):
                    pool.wait_ge(taps_merged, l * NC + c + 1)
                    if c > 1:
                        pool.wait_ge(channels_added, l * (NC - 1) + c - 1)
                    nc.gpsimd.tensor_tensor(channel_sum[:], y_conv[:, 0, :] if c == 1 else channel_sum[:],
                                            y_conv[:, c, :], ALU.add).then_inc(channels_added, 1)

                def add_channel_squares():
                    for c in range(1, NC):
                        pool.wait_ge(y_squared, l * 3 * NC + c + 1)
                        if c > 1:
                            pool.wait_ge(squares_added, l * (NC - 1) + c - 1)
                        nc.gpsimd.tensor_tensor(channel_squares[:, 0, :], channel_squares[:, 0, :],
                                                channel_squares[:, c, :], ALU.add).then_inc(squares_added, 1)

                done = 0
                for t in range(12):
                    mix_low(t)
                    if t >= 2:
                        add_products(done, P_SPREAD[t - 2])
                        done += P_SPREAD[t - 2]
                mix_low(12)
                mix_low(13)
                diagonals(0)
                add_products(done, P_SPREAD[10])
                done += P_SPREAD[10]
                for g in range(N_GROUPS - 1):
                    add_products(done, 1)
                    diagonals(g + 1)
                    add_products(done + 1, P_SPREAD[11 + g] - 1)
                    done += P_SPREAD[11 + g]
                    if g == 1:
                        add_channel(1)
                    elif g == 4:
                        add_channel(2)
                add_channel_squares()
                mix_low(14)
                mix_low(15)
                for s in range(4):
                    low(l, MIX_S + 16 + s + RING, s % RING)
                    for m in (2 * s, 2 * s + 1):
                        pool.wait_ge(evicted, turn_no(l, MIX_T + OUT_A_TURN + m) + 1 + BANKS)
                        nc.gpsimd.tensor_tensor(x[:, m, :], x[:, m, :], work[:, m % BANKS, :],
                                                ALU.add).then_inc(x_half, 1)
                for s in range(4):
                    for m in (2 * s, 2 * s + 1):
                        add_square(prep_no(l, 2), m, first=m == 0, of=x_square[m % 2])
                    low(l, MIX_S + 20 + s + RING, s % RING)
                ffn_steps(l, FFN_SLOTS + MIX_SLOTS, prep_no(l, 3), last=True)
            add_square(prep_no(DEPTH, 0), ND - 1)
            pool.wait_ge(rstd_copied, DEPTH + 1)
            for m in range(FINAL_SPLIT, ND):
                pool.wait_ge(gained, FINAL_ORDER.index(m) + 1)
                nc.gpsimd.tensor_tensor(result[:, m, :], result[:, m, :], rstd[:], ALU.mult).then_inc(result_p, 1)

        @block.scalar
        def _(act):
            def high(l, n, r, uses):
                act.wait_ge(landed[r], uses * 16 + 16)
                act.wait_ge(used, slot_no(l, n) + 1)
                nc.scalar.activation(w_hi[:, r, :], stage[:, r, :], ACT.Copy).then_inc(hi_made, 1)

            def uses_of(l, n, r):
                return l * (LAYER_SLOTS // RING) + n

            def root(l, name, by_token=False):
                act.wait_ge(stat_made, stat_no(l, name) + 1)
                act.wait_ge(rstd_made, root_no(l, name) + 1)
                to, source = (std_token[:], stat_bank[name][:, 0:NB]) if by_token else (std[:], stat_bank[name][:])
                count = D_CONV if name in ("attn", "var", "conv") else D_MODEL
                nc.scalar.activation(to, source, ACT.Sqrt, bias=eps[:], scale=1.0 / count).then_inc(std_made, 1)

            def ffn_steps(l, base, turns, name, last):
                root(l, name)
                with act.Fori(0, NF // 2) as i:
                    for j in range(2):
                        f = i * 2 + j
                        high(l, base + f * 2 + RING, 2 * j, uses_of(l, base // RING + 1 + i, 0))
                        act.wait_ge(evicted, turn_no(l, turns + f * 2) + 1 + BANKS)
                        nc.scalar.activation(work[:, 2 * j, :], work[:, 2 * j, :], ACT.Silu).then_inc(silu_made, 1)
                        high(l, base + f * 2 + 1 + RING, 2 * j + 1, uses_of(l, base // RING + 1 + i, 0))
                at = base + 2 * NF

                def down(m):
                    for j in range(4):
                        high(l, at + m * 4 + RING + j, j, uses_of(l, at // RING + 1 + m, 0))

                with act.Fori(0, ND - 1) as m:
                    down(m)
                if not last:
                    down(ND - 1)

            act.dma_start(gain0[:], first_gain).then_inc(gain_landed, 16)
            for i in range(4):
                act.dma_start(x[:, 2 * i:2 * i + 2, :],
                              xT.rearrange("(k p) n -> p k n", p=P)[:, 2 * i:2 * i + 2, :]).then_inc(x_landed[i], 16)
            act.wait_ge(small_made, 1)
            with act.Fori(0, DEPTH) as l:
                for j in range(RING):
                    high(l, j, j, uses_of(l, 0, 0))
                ffn_steps(l, 0, 0, "ffn1", last=False)

                def mix_high(s):
                    high(l, MIX_S + s + RING, s % RING, uses_of(l, (MIX_S + s) // RING + 1, 0))

                def tile_ready(t):
                    act.wait_ge(evicted, turn_no(l, MIX_T + t) + 1 + BANKS)

                def gate_tanh(t):
                    tile_ready(t)
                    nc.scalar.activation(work[:, t % BANKS, :], work[:, t % BANKS, :], ACT.Tanh,
                                         scale=0.5).then_inc(tanh_made, 1)

                def exp_scores(g, c):
                    b, kv = divmod(g, 2)
                    n = keys_of(b)[1] * P
                    unit = probs[g % PROBS][:, c, 0:n]
                    act.wait_ge(att_freed, l * len(ATT) + ATT["scores", g, c] + 1)
                    nc.scalar.activation(unit, unit, ACT.Exp, bias=neg_max[:, g % PROBS, c:c + 1], scale=-1.0,
                                         accum_out=p_sum[:, g % PROBS, c:c + 1]).then_inc(exped, 1)

                def exp_sink(g):
                    act.wait_ge(sink_ready, l * N_GROUPS + g + 1)
                    nc.scalar.activation(sink_exp[:, g % PROBS, :], sink_arg[:, g % PROBS, :], ACT.Exp).then_inc(sink_exped, 1)

                def evict_o(g):
                    b, kv = divmod(g, 2)
                    rows = slice(HEAD_DIM * kv, HEAD_DIM * (kv + 1))
                    act.wait_ge(o_made, l * N_GROUPS + g + 1)
                    nc.scalar.activation(y_attn[rows, :, b * P:(b + 1) * P],
                                         side_bank[rows, :].rearrange("p (c q) -> p c q", q=P),
                                         ACT.Copy).then_inc(o_evicted, 1)

                def products(first, count):
                    for n in range(first, first + count):
                        c, t = n // P_TAPS, V_TAPS + n % P_TAPS
                        if n >= 3:
                            act.wait_ge(tap_added, l * NC * P_TAPS + n - 2)
                        act.wait_ge(glu_made, l * NC + c + 1)
                        at = CONV_W + c * CONV_WIDTH + t
                        nc.scalar.activation(product[n % 3][:], glu[:, c, t:t + SEQ], ACT.Copy,
                                             scale=par[:, at:at + 1]).then_inc(tap_product, 1)

                def turned_high(g, c):
                    n = keys_of(g // 2)[1]
                    act.wait_ge(turned, l * N_UNITS + g * GROUP + c + 1)
                    if g >= 2 and c == 0:
                        act.wait_ge(o_made, l * N_GROUPS + g - 1)
                    src = att_bank[ATT["turned", g, c] % ATT_BANKS][:, 0:n * P].rearrange("p (k q) -> p k q", q=P)
                    nc.scalar.activation(pt_hi[:, g % 2, 0:n, c, :], src, ACT.Copy).then_inc(pt_hi_made, 1)

                root(l, "mix")
                done = 0
                for t in range(12):
                    mix_high(t)
                    name = IN_TILES[t]
                    if name[0] == "g":
                        gate_tanh(t)
                    elif name == "k":
                        tile_ready(t)
                        nc.scalar.activation(k_hi[:], work[:, t % BANKS, :], ACT.Copy).then_inc(qk_hi, 1)
                    elif name[0] == "q":
                        c = int(name[1])
                        tile_ready(t)
                        nc.scalar.activation(q_hi[:, c, :], work[:, t % BANKS, :], ACT.Copy).then_inc(qk_hi, 1)
                        if c == 0:
                            act.wait_ge(v_turned, l + 1)
                            nc.scalar.activation(v_hi[:].rearrange("p b d -> p (b d)"), side_bank[:],
                                                 ACT.Copy).then_inc(v_hi_made, 1)
                    if t >= 2:
                        products(done, P_SPREAD[t - 2])
                        done += P_SPREAD[t - 2]
                mix_high(12)
                mix_high(13)
                for c in range(GROUP):
                    exp_scores(0, c)
                exp_sink(0)
                products(done, 1)
                exp_scores(1, 0)
                exp_scores(1, 1)
                gate_tanh(13)
                products(done + 1, 1)
                exp_scores(1, 2)
                exp_scores(1, 3)
                exp_sink(1)
                done += P_SPREAD[10]
                for g in range(N_GROUPS):
                    p = P_SPREAD[11 + g] if g + 1 < N_GROUPS else 0
                    for c in range(GROUP):
                        turned_high(g, c)
                        if c and g + AHEAD < N_GROUPS:
                            exp_scores(g + AHEAD, c - 1)
                        elif c == 0 and g and g + 1 < N_GROUPS:
                            exp_scores(g + 1, GROUP - 1)
                            exp_sink(g + 1)
                        if c in PRODUCT_HEADS[p]:
                            products(done, 1)
                            done += 1
                    if g:
                        evict_o(g - 1)

                def square_channels(c):
                    act.wait_ge(centred, l * NC + c + 1)
                    nc.scalar.activation(channel_squares[:, c, :], y_conv[:, c, :], ACT.Square).then_inc(y_squared, 1)

                def high_attention(c):
                    nc.scalar.activation(xs_hi[:, c, :], y_attn[:, c, :], ACT.Copy,
                                         scale=par[:, G_ATTN + c:G_ATTN + c + 1]).then_inc(y_hi_made, 1)

                square_channels(0)
                square_channels(1)
                evict_o(N_GROUPS - 1)
                act.wait_ge(o_evicted, l * N_GROUPS + N_GROUPS)
                for c in range(NC):
                    high_attention(c)
                square_channels(2)
                square_channels(3)
                for c in range(NC):
                    nc.scalar.activation(squares[:, c, :], y_attn[:, c, :], ACT.Square).then_inc(y_squared, 1)
                mix_high(14)
                root(l, "var", by_token=True)
                root(l, "attn", by_token=True)
                mix_high(15)
                mix_high(16)
                for c in range(NC):
                    act.wait_ge(ln_scaled, l * NC + c + 1)
                    nc.scalar.activation(y_conv[:, c, :], y_conv[:, c, :], ACT.Silu,
                                         bias=par[:, LN_B + c:LN_B + c + 1],
                                         scale=par[:, LN_G + c:LN_G + c + 1]).then_inc(ln_silu, 1)
                    act.wait_ge(ln_silu, l * NC + c + 1)
                    nc.scalar.activation(y_hi[:, c, :], y_conv[:, c, :], ACT.Copy,
                                         scale=par[:, G_CONV + c:G_CONV + c + 1]).then_inc(y_hi_made, 1)
                mix_high(17)
                for c in range(NC):
                    nc.scalar.activation(squares[:, c, :], y_conv[:, c, :], ACT.Square).then_inc(y_squared, 1)
                mix_high(18)
                root(l, "conv")
                mix_high(19)
                for m in range(ND):
                    act.wait_ge(x_made, l * ND + m + 1)
                    nc.scalar.activation(xs_hi[:, m, :], x[:, m, :], ACT.Copy,
                                         scale=par[:, G_FFN2 + m:G_FFN2 + m + 1]).then_inc(x_hi_made, 1)
                    act.wait_ge(sq_added, prep_no(l, 2) * ND + max(m - 1, 0))
                    nc.scalar.activation(x_square[m % 2][:], x[:, m, :], ACT.Square).then_inc(squared, 1)
                    if m % 2:
                        mix_high(20 + m // 2)
                ffn_steps(l, FFN_SLOTS + MIX_SLOTS, FFN_TURNS + MIX_TURNS, "ffn2", last=True)
            root(DEPTH, "ffn1", by_token=True)

        @block.vector
        def _(dve):
            dve.sem_inc(evicted, BANKS)
            dve.sem_inc(rstd_made, 1)
            nc.vector.memset(ones[:], 1.0).then_inc(consts_v, 1)
            dve.wait_ge(consts_p, 1)
            nc.vector.tensor_copy(dist[:], dist_int[:]).then_inc(consts_v, 1)
            dve.wait_ge(consts_v, 2)
            nc.vector.tensor_scalar(dist_neg[:], dist[:], -1.0, None, ALU.mult)
            nc.vector.memset(eps[:], EPS)
            nc.vector.memset(zero[:], 0.0)
            for c in range(NC):
                for kv in range(N_KV_HEADS):
                    nc.vector.memset(q_scale[HEAD_DIM * kv:HEAD_DIM * (kv + 1), c:c + 1],
                                     -1.0 / (math.sqrt(HEAD_DIM) * slope(kv, c)))
            dve.drain().then_inc(small_made, 1)
            dve.wait_ge(small_made, 1)
            nc.vector.tensor_tensor(dist[:], dist[:], dist_neg[:], ALU.max).then_inc(consts_v, 1)

            def split_x(prep, m, gain, gain_at):
                dve.wait_ge(x_hi_made, prep * ND + m + 1)
                nc.vector.scalar_tensor_tensor(chunk(xs_lo, m), chunk(x, m), column(gain, gain_at + m),
                                               chunk(xs_hi, m).bitcast(F32), ALU.mult,
                                               ALU.subtract).then_inc(x_split, 1)

            def recip(l, name):
                dve.wait_ge(std_made, root_no(l, name) + 1)
                nc.vector.reciprocal(rstd[:], std[:]).then_inc(rstd_made, 1)

            def rstd_ready(l, name):
                dve.wait_ge(rstd_made, root_no(l, name) + 2)

            def token_recip(l, name):
                dve.wait_ge(std_made, root_no(l, name) + 1)
                nc.vector.reciprocal(rstd_token[:, int(name != "var"), :], std_token[:]).then_inc(rstd_made, 1)

            def take_rstd(copy, spread_value, name):
                dve.wait_ge(spread, spread_value)
                nc.vector.tensor_copy(rstd[:], stat_bank[name][:]).then_inc(rstd_copied, 1)
                dve.wait_ge(rstd_copied, copy + 1)

            def tile_summed(l, slot):
                dve.wait_ge(used, slot_no(l, slot) + 1 + RING)

            def scale_tile(b, w, inc=1):
                nc.vector.tensor_tensor(work[:, w, :], bank[b][:], rstd[:], ALU.mult).then_inc(evicted, inc)

            def own(l, turn):
                dve.wait_ge(evicted, turn_no(l, turn) + 1 + BANKS)

            def ffn_steps(l, base, turns, h_base, prep, name, gain_at):
                recip(l, name)
                with dve.Fori(0, NF // 2) as i:
                    rstd_ready(l, name)
                    for j in range(2):
                        f = i * 2 + j
                        h_no = l * 2 * NF + h_base + f
                        for part in (2 * j, 2 * j + 1):
                            tile_summed(l, base + i * 4 + part)
                            scale_tile(part, part)
                        own(l, turns + f * 2 + 1)
                        dve.wait_ge(silu_made, h_no + 1)
                        nc.vector.tensor_tensor(work[:, 2 * j + 1, :], work[:, 2 * j, :], work[:, 2 * j + 1, :],
                                                ALU.mult).then_inc(h_made, 1)
                        dve.wait_ge(h_made, h_no + 1)
                        nc.vector.tensor_scalar(chunk(h_hi, f), work[:, 2 * j + 1, :], 1.0, None,
                                                ALU.mult).then_inc(h_hi_made, 1)
                        dve.wait_ge(h_hi_made, h_no + 1)
                        nc.vector.tensor_tensor(chunk(h_lo, f), work[:, 2 * j + 1, :], chunk(h_hi, f).bitcast(F32),
                                                ALU.subtract).then_inc(h_split, 1)
                with dve.Fori(0, ND // 4) as i:
                    dve.wait_ge(par_landed, l * 16 + 16)
                    for j in range(4):
                        m = i * 4 + j
                        tile_summed(l, base + 2 * NF + m * 4 + 3)
                        nc.vector.scalar_tensor_tensor(chunk(x, m), bank[j][:], 0.5, chunk(x, m), ALU.mult,
                                                       ALU.add).then_inc(evicted, 1)
                        own(l, turns + 2 * NF + m)
                        dve.wait_ge(sq_added, prep * ND + m)
                        nc.vector.tensor_tensor(sq[:], chunk(x, m), chunk(x, m), ALU.mult).then_inc(squared, 1)
                        high_x(m, par, gain_at)
                        split_x(prep, m, par, gain_at)

            def high_x(m, gain, gain_at):
                nc.vector.tensor_scalar(chunk(xs_hi, m), chunk(x, m), column(gain, gain_at + m), None,
                                        ALU.mult).then_inc(x_hi_made, 1)

            dve.wait_ge(gain_landed, 16)
            for m in range(ND):
                if m % 2 == 0:
                    dve.wait_ge(x_landed[m // 2], 16)
                high_x(m, gain0, 0)
                split_x(0, m, gain0, 0)
            for m in range(ND):
                to = x_squares[:, m, :] if m < ND - 1 else sq[:]
                nc.vector.tensor_tensor(to, x[:, m, :], x[:, m, :], ALU.mult).then_inc(squared, 1)
            for m in range(1, ND - 1):
                dve.wait_ge(squared, m + 1)
                if m > 1:
                    dve.wait_ge(sq_added, m)
                nc.vector.tensor_tensor(sq_sum[:], x_squares[:, 0, :] if m == 1 else sq_sum[:], x_squares[:, m, :],
                                        ALU.add).then_inc(sq_added, 2 if m == 1 else 1)
            with dve.Fori(0, DEPTH) as l:
                ffn_steps(l, 0, 0, 0, prep_no(l, 1), "ffn1", G_MIX)

                def turn(t):
                    return MIX_T + t

                def in_summed(t):
                    tile_summed(l, MIX_S + (t if t < 12 else 13 + 2 * (t - 12)))

                def tile(t, inc=1):
                    in_summed(t)
                    if IN_TILES[t][0] == "a":
                        nc.vector.scalar_tensor_tensor(work[:, t % BANKS, :], bank[t % BANKS][:], 0.5, rstd[:],
                                                       ALU.mult, ALU.mult).then_inc(evicted, inc)
                    else:
                        scale_tile(t % BANKS, t % BANKS, inc)

                def out_summed(slot, m):
                    if m % 2:
                        tile_summed(l, MIX_S + slot + m // 2)
                    else:
                        dve.wait_ge(half_used, l * ND + (slot - 16) + m // 2 + 1)

                def gate(c):
                    ta, tg = IN_TILES.index(f"a{c}"), IN_TILES.index(f"g{c}")
                    own(l, turn(ta))
                    dve.wait_ge(tanh_made, l * NC + c + 1)
                    nc.vector.scalar_tensor_tensor(glu[:, c, CONV_PAD:CONV_PAD + SEQ], work[:, tg % BANKS, :], 1.0,
                                                   work[:, ta % BANKS, :], ALU.add, ALU.mult).then_inc(glu_made, 1)

                def taps(first, count):
                    for n in range(first, first + count):
                        c, t = divmod(n, V_OPS)
                        if t == 0:
                            dve.wait_ge(glu_made, l * NC + c + 1)
                        if t < V_TAPS:
                            h = glu[:, c, t:t + SEQ]
                            w = par[:, CONV_W + c * CONV_WIDTH + t:CONV_W + c * CONV_WIDTH + t + 1]
                        into = y_conv[:, c, :] if t % 2 == 0 else odd_taps[:]
                        if t >= 2 or (c and t == 1):
                            dve.wait_ge(tapped, l * NC * V_OPS + n - (t < V_TAPS))
                        if t == V_TAPS:
                            nc.vector.tensor_tensor(y_conv[:, c, :], y_conv[:, c, :], odd_taps[:],
                                                    ALU.add).then_inc(tapped, 1)
                        elif t == 0:
                            nc.vector.tensor_scalar(into, h, w, par[:, CONV_B + c:CONV_B + c + 1], ALU.mult,
                                                    ALU.add).then_inc(tapped, 1)
                        elif t == 1:
                            nc.vector.tensor_scalar(into, h, w, None, ALU.mult).then_inc(tapped, 1)
                        else:
                            nc.vector.scalar_tensor_tensor(into, h, w, into, ALU.mult, ALU.add).then_inc(tapped, 1)

                def merge(c):
                    dve.wait_ge(tapped, (l * NC + c + 1) * V_OPS)
                    dve.wait_ge(tap_added, (l * NC + c + 1) * P_TAPS)
                    nc.vector.tensor_tensor(y_conv[:, c, :], y_conv[:, c, :], pool_taps[:],
                                            ALU.add).then_inc(taps_merged, 1)

                def low_qk(t, n, hi, lo):
                    own(l, turn(t))
                    dve.wait_ge(qk_hi, l * (NC + 1) + n + 1)
                    nc.vector.tensor_tensor(lo, work[:, t % BANKS, :], hi.bitcast(F32),
                                            ALU.subtract).then_inc(qk_split, 1)

                def bias_scores(g, c, first_tap, n_taps):
                    b, kv = divmod(g, 2)
                    first, n = keys_of(b)
                    at = (first - (b - 1)) * P
                    k = ATT["scores", g, c]
                    if g == 0:
                        dve.wait_ge(consts_p, 5)
                    if g == PROBS - 1:
                        dve.wait_ge(glu_made, l * NC + NC)
                    dve.wait_ge(scored, l * N_UNITS + g * GROUP + c + 1)
                    if g >= PROBS:
                        dve.wait_ge(turned, l * N_UNITS + (g - PROBS) * GROUP + c + 1)
                    taps(first_tap, n_taps)
                    nc.vector.tensor_tensor_reduce(
                        out=probs[g % PROBS][:, c, 0:n * P], in0=att_bank[k % ATT_BANKS][:, 0:n * P],
                        in1=dist[:, at:at + n * P], scale=slope(kv, c),
                        scalar=neg_sink[:, kv * GROUP + c:kv * GROUP + c + 1], op0=ALU.add, op1=ALU.min,
                        accum_out=neg_max[:, g % PROBS, c:c + 1]).then_inc(att_freed, 1)

                def sink_args(g):
                    kv = g % 2
                    dve.wait_ge(att_freed, l * len(ATT) + ATT["scores", g, GROUP - 1] + 1)
                    nc.vector.tensor_tensor(sink_arg[:, g % PROBS, :], neg_max[:, g % PROBS, :],
                                            par[:, SINK + kv * GROUP:SINK + (kv + 1) * GROUP],
                                            ALU.add).then_inc(sink_ready, 1)

                def denominators(g):
                    dve.wait_ge(sink_exped, l * N_GROUPS + g + 1)
                    dve.wait_ge(exped, l * N_UNITS + g * GROUP + GROUP)
                    nc.vector.tensor_tensor(den[:, g % PROBS, :], p_sum[:, g % PROBS, :], sink_exp[:, g % PROBS, :],
                                            ALU.add).then_inc(den_made, 1)
                    dve.wait_ge(den_made, l * N_GROUPS + g + 1)
                    nc.vector.reciprocal(r_den[:, g % PROBS, :], den[:, g % PROBS, :]).then_inc(r_den_made, 1)

                def turned_low(g, c):
                    n = keys_of(g // 2)[1]
                    dve.wait_ge(pt_hi_made, l * N_UNITS + g * GROUP + c + 1)
                    src = att_bank[ATT["turned", g, c] % ATT_BANKS][:, 0:n * P].rearrange("p (k q) -> p k q", q=P)
                    nc.vector.tensor_tensor(pt_lo[:, g % 2, 0:n, c, :], src, pt_hi[:, g % 2, 0:n, c, :].bitcast(F32),
                                            ALU.subtract).then_inc(att_freed, 1)

                nc.vector.memset(glu[:, :, 0:CONV_PAD], 0.0).then_inc(padded, 1)
                nc.vector.memset(glu[:, :, CONV_PAD + SEQ:], 0.0).then_inc(padded, 1)
                nc.vector.tensor_scalar(neg_sink[:], par[:, SINK:SINK + N_Q_HEADS], -1.0, None,
                                        ALU.mult).then_inc(neg_sink_made, 1)
                dve.wait_ge(padded, l * 2 + 2)
                dve.wait_ge(neg_sink_made, l + 1)
                recip(l, "mix")
                rstd_ready(l, "mix")
                tile(0)
                tile(1)
                gate(0)
                done = 0
                for t in range(2, 12):
                    name = IN_TILES[t]
                    if name[0] == "q":
                        c = int(name[1])
                        in_summed(t)
                        nc.vector.scalar_tensor_tensor(work[:, t % BANKS, :], bank[t % BANKS][:], q_scale[:, c:c + 1],
                                                       rstd[:], ALU.mult, ALU.mult).then_inc(evicted, 1)
                    else:
                        tile(t)
                    taps(done, V_SPREAD[t - 2])
                    done += V_SPREAD[t - 2]
                    if name[0] == "g":
                        gate(int(name[1]))
                    elif name == "k":
                        low_qk(t, 0, k_hi[:], k_lo[:])
                    elif name == "v":
                        merge(0)
                    elif name[0] == "q":
                        low_qk(t, 1 + c, q_hi[:, c, :], q_lo[:, c, :])
                        if c == 0:
                            dve.wait_ge(v_hi_made, l + 1)
                            nc.vector.tensor_tensor(v_lo[:].rearrange("p b d -> p (b d)"), side_bank[:],
                                                    v_hi[:].rearrange("p b d -> p (b d)").bitcast(F32),
                                                    ALU.subtract).then_inc(v_split, 1)
                tile(12)
                for c in range(GROUP):
                    bias_scores(0, c, done, 1)
                    done += 1
                sink_args(0)
                for c in range(GROUP):
                    bias_scores(1, c, done, 1)
                    done += 1
                    if c == 0:
                        denominators(0)
                    elif c == 1:
                        tile(13, inc=3)
                sink_args(1)
                gate(3)
                merge(1)
                for g in range(N_GROUPS):
                    for c in range(GROUP):
                        turned_low(g, c)
                        if g + AHEAD < N_GROUPS:
                            bias_scores(g + AHEAD, c, done, 1)
                            done += 1
                        if c == 0 and g + 1 < N_GROUPS:
                            denominators(g + 1)
                        if (g, c) in MERGED_AT:
                            merge(MERGED_AT[g, c])
                        if (g, c) == (N_GROUPS - 1, 0):
                            dve.wait_ge(taps_merged, l * NC + NC)
                            dve.wait_ge(channels_added, l * (NC - 1) + NC - 2)
                            nc.vector.tensor_tensor(channel_sum[:], channel_sum[:], y_conv[:, NC - 1, :],
                                                    ALU.add).then_inc(channels_added, 1)
                    if g + AHEAD < N_GROUPS:
                        sink_args(g + AHEAD)
                assert done == NC * V_OPS, done

                def out_a(m):
                    if m >= BANKS:
                        dve.wait_ge(x_half, l * ND + m - BANKS + 1)
                    out_summed(16, m)
                    scale_tile(m % BANKS, m % BANKS)

                def centre(c):
                    nc.vector.scalar_tensor_tensor(y_conv[:, c, :], stat_bank["mean"][:], -1.0 / D_CONV,
                                                   y_conv[:, c, :], ALU.mult, ALU.add).then_inc(centred, 1)

                def split_attention(c):
                    dve.wait_ge(y_hi_made, l * 2 * NC + c + 1)
                    nc.vector.scalar_tensor_tensor(xs_lo[:, c, :], y_attn[:, c, :], par[:, G_ATTN + c:G_ATTN + c + 1],
                                                   xs_hi[:, c, :].bitcast(F32), ALU.mult,
                                                   ALU.subtract).then_inc(y_split, 1)

                def sum_squares(n):
                    for c in range(1, NC):
                        dve.wait_ge(y_squared, (l * 3 + 1 + n) * NC + c + 1)
                        if c > 1:
                            dve.wait_ge(result_added, (l * 2 + n) * (NC - 1) + c - 1)
                        nc.vector.tensor_tensor(squares[:, 0, :], squares[:, 0, :], squares[:, c, :],
                                                ALU.add).then_inc(result_added, 1)

                def scale_channels(c):
                    dve.wait_ge(y_squared, l * 3 * NC + c + 1)
                    nc.vector.tensor_tensor(y_conv[:, c, :], y_conv[:, c, :], stat_bank["var"][:],
                                            ALU.mult).then_inc(ln_scaled, 1)

                dve.wait_ge(stat_made, stat_no(l, "mean") + 1)
                for c in range(NC):
                    centre(c)
                for c in range(NC):
                    split_attention(c)
                sum_squares(0)
                token_recip(l, "var")
                token_recip(l, "attn")
                dve.wait_ge(spread, spread_no(l, "var") + 1)
                scale_channels(0)
                take_rstd(l, spread_no(l, "attn") + 1, "attn")
                out_a(0)
                scale_channels(1)
                scale_channels(2)
                out_a(1)
                scale_channels(3)
                for m in range(2, 5):
                    out_a(m)
                for c in range(NC):
                    dve.wait_ge(y_hi_made, l * 2 * NC + NC + c + 1)
                    nc.vector.scalar_tensor_tensor(y_lo[:, c, :], y_conv[:, c, :],
                                                   par[:, G_CONV + c:G_CONV + c + 1],
                                                   y_hi[:, c, :].bitcast(F32), ALU.mult,
                                                   ALU.subtract).then_inc(y_split, 1)
                out_a(5)
                sum_squares(1)
                out_a(6)
                out_a(7)
                own(l, turn(OUT_A_TURN + ND - 1))
                recip(l, "conv")
                rstd_ready(l, "conv")
                for m in range(ND):
                    out_summed(20, m)
                    if m < BANKS:
                        dve.wait_ge(x_half, l * ND + BANKS + m + 1)
                    scale_tile(m % BANKS, m % BANKS)
                    own(l, turn(OUT_C_TURN + m))
                    nc.vector.tensor_tensor(x[:, m, :], x[:, m, :], work[:, m % BANKS, :],
                                            ALU.add).then_inc(x_made, 1)
                    if m:
                        dve.wait_ge(x_made, l * ND + m)
                        split_x(prep_no(l, 2), m - 1, par, G_FFN2)
                dve.wait_ge(x_made, l * ND + ND)
                split_x(prep_no(l, 2), ND - 1, par, G_FFN2)
                ffn_steps(l, FFN_SLOTS + MIX_SLOTS, FFN_TURNS + MIX_TURNS, NF, prep_no(l, 3), "ffn2", G_NEXT)

            for n, m in enumerate(FINAL_ORDER):
                if n == 5:
                    token_recip(DEPTH, "ffn1")
                nc.vector.tensor_scalar(result[:, m, :], x[:, m, :], par[:, G_NEXT + m:G_NEXT + m + 1], None,
                                        ALU.mult).then_inc(gained, 1)
            take_rstd(DEPTH, spread_no(DEPTH, "var") + 1, "ffn1")
            for m in range(FINAL_SPLIT):
                dve.wait_ge(gained, FINAL_ORDER.index(m) + 1)
                nc.vector.tensor_tensor(result[:, m, :], result[:, m, :], rstd[:], ALU.mult).then_inc(result_v, 1)

        @block.tensor
        def _(pe):
            pe.sem_inc(used, RING)

            def triple(to, wh, wl, mh, ml, first, last):
                nc.tensor.matmul(to, wh, mh, start=first, stop=False)
                nc.tensor.matmul(to, wh, ml, start=False, stop=False)
                return nc.tensor.matmul(to, wl, mh, start=False, stop=last)

            def weights(r, i):
                at = slice(i * P, (i + 1) * P)
                return w_hi[:, r, at], w_lo[:, r, at]

            def take(l, n):
                pe.wait_ge(split, slot_no(l, n) + 1 + RING)

            def open_bank(l, turn):
                pe.wait_ge(evicted, turn_no(l, turn) + 1)

            def statistic(name, of):
                nc.tensor.matmul(stat_bank[name][:], ones[:], of, start=True, stop=True).then_inc(stat_made, 1)

            def x_statistic(l, name):
                pe.wait_ge(sq_added, l * 3 * ND + {"ffn1": ND, "mix": 2 * ND, "ffn2": 3 * ND}[name])
                statistic(name, sq_sum[:])

            def sum_tokens(to, of):
                for b in range(NB):
                    last = nc.tensor.matmul(to[:, b:b + 1], of[:, b * P:(b + 1) * P], ones[:, 0:1],
                                            start=True, stop=True)
                last.then_inc(stat_made, 1)

            def spread_factors(l, name):
                pe.wait_ge(rstd_made, root_no(l, name) + 2)
                to, factors = stat_bank[name], rstd_token[:, int(name != "var"), :]
                for b in range(NB):
                    last = nc.tensor.matmul(to[:, b * P:(b + 1) * P], factors[:, b:b + 1].to_broadcast([P, P]),
                                            ident[:], start=True, stop=True)
                last.then_inc(spread, 1)

            def model_tile(l, n, r, turn, b, prep=None, part=(0, ND), between=None):
                first, end = part
                take(l, n)
                if first == 0:
                    open_bank(l, turn)
                for k in range(first, end):
                    if prep is not None:
                        pe.wait_ge(x_split, prep * ND + k + 1)
                    last = triple(bank[b][:], *weights(r, k - first), xs_hi[:, k, :], xs_lo[:, k, :], k == 0,
                                  k == ND - 1)
                    if k == end - 1:
                        last.then_inc(used, 1)
                    if between and k in between:
                        between[k]()

            def ffn_steps(l, base, turns, h_base, prep, name):
                for j in range(4):
                    model_tile(l, base + j, j, turns + j, j, prep if j == 0 else None,
                               between={3: lambda: x_statistic(l, name)} if j == 2 else None)
                with pe.Fori(1, NF // 2) as i:
                    for j in range(4):
                        model_tile(l, base + i * 4 + j, j, turns + i * 4 + j, j)
                with pe.Fori(0, ND // 4) as i:
                    for j in range(4):
                        turn = turns + 2 * NF + i * 4 + j
                        open_bank(l, turn)
                        f = 0
                        for s, count in enumerate(DOWN):
                            take(l, base + 2 * NF + (i * 4 + j) * 4 + s)
                            pe.wait_ge(h_split, l * 2 * NF + h_base + f + count)
                            for k in range(count):
                                last = triple(bank[j][:], *weights(s, k), h_hi[:, f, :], h_lo[:, f, :], f == 0,
                                              f == NF - 1)
                                f += 1
                            last.then_inc(used, 1)

            pe.wait_ge(consts_v, 1)
            pe.wait_ge(consts_p, 3)
            with pe.Fori(0, DEPTH) as l:
                ffn_steps(l, 0, 0, 0, prep_no(l, 0), "ffn1")

                def in_tile(t, between=None):
                    model_tile(l, MIX_S + t, t % RING, MIX_T + t, t % BANKS, prep_no(l, 1) if t == 0 else None,
                               between=between)

                def half_tile(t, half):
                    s = 12 + 2 * (t - 12) + half
                    model_tile(l, MIX_S + s, s % RING, MIX_T + t, t % BANKS, part=(4 * half, 4 * half + 4))

                def scores(g, c):
                    b, kv = divmod(g, 2)
                    first, n = keys_of(b)
                    k = ATT["scores", g, c]
                    rows = slice(HEAD_DIM * kv, HEAD_DIM * (kv + 1))
                    q, keys = slice(b * P, (b + 1) * P), slice(first * P, (first + n) * P)
                    to = att_bank[k % ATT_BANKS][:, 0:n * P]
                    if k >= ATT_BANKS:
                        pe.wait_ge(att_freed, l * len(ATT) + k - ATT_BANKS + 1)
                    elif k >= 3:
                        pe.wait_ge(evicted, turn_no(l, MIX_T + 12) + 1 + BANKS)
                    nc.tensor.matmul(to, q_hi[rows, c, q], k_hi[rows, keys], start=True, stop=False)
                    nc.tensor.matmul(to, q_hi[rows, c, q], k_lo[rows, keys], start=False, stop=False)
                    nc.tensor.matmul(to, q_lo[rows, c, q], k_hi[rows, keys], start=False,
                                     stop=True).then_inc(scored, 1)

                def turn_weights(g, c):
                    n = keys_of(g // 2)[1]
                    k = ATT["turned", g, c]
                    pe.wait_ge(exped, l * N_UNITS + g * GROUP + c + 1)
                    pe.wait_ge(diag_made, l * N_UNITS + g * GROUP + c + 1)
                    pe.wait_ge(att_freed, l * len(ATT) + k - ATT_BANKS + 1)
                    for i in range(n):
                        last = nc.tensor.matmul(att_bank[k % ATT_BANKS][:, i * P:(i + 1) * P],
                                                probs[g % PROBS][:, c, i * P:(i + 1) * P], diag[:, c, :],
                                                start=True, stop=True)
                    last.then_inc(turned, 1)

                def weigh_values(g):
                    first, n = keys_of(g // 2)
                    pe.wait_ge(att_freed, l * len(ATT) + ATT["turned", g, GROUP - 1] + 1)
                    if g:
                        pe.wait_ge(o_evicted, l * N_GROUPS + g)
                    for i in range(n):
                        mh = pt_hi[:, g % 2, i, :, :].rearrange("p c q -> p (c q)")
                        ml = pt_lo[:, g % 2, i, :, :].rearrange("p c q -> p (c q)")
                        last = triple(side_bank[:], v_hi[:, first + i, :], v_lo[:, first + i, :], mh, ml, i == 0,
                                      i == n - 1)
                    last.then_inc(o_made, 1)

                def out_tiles(first_slot, first_turn, hi, lo, done, between):
                    for m in range(ND):
                        s = first_slot + m // 2
                        if m % 2 == 0:
                            take(l, MIX_S + s)
                        open_bank(l, MIX_T + first_turn + m)
                        if m == 0:
                            for c in range(NC):
                                pe.wait_ge(y_hi_made, l * 2 * NC + done + c + 1)
                                wh, wl = weights(s % RING, c)
                                nc.tensor.matmul(bank[0][:], wh, hi[:, c, :], start=c == 0, stop=False)
                                nc.tensor.matmul(bank[0][:], wl, hi[:, c, :], start=False, stop=False)
                        for c in range(NC):
                            if m == 0:
                                pe.wait_ge(y_split, l * 2 * NC + done + c + 1)
                                last = nc.tensor.matmul(bank[0][:], weights(s % RING, c)[0], lo[:, c, :],
                                                        start=False, stop=c == NC - 1)
                            else:
                                last = triple(bank[m % BANKS][:], *weights(s % RING, 4 * (m % 2) + c),
                                              hi[:, c, :], lo[:, c, :], c == 0, c == NC - 1)
                            if c == NC - 1:
                                last.then_inc(used if m % 2 else half_used, 1)
                            if (m, c) in between:
                                between[m, c]()

                def token_statistics():
                    pe.wait_ge(squares_added, (l + 1) * (NC - 1))
                    sum_tokens(stat_bank["var"], channel_squares[:, 0, :])
                    pe.wait_ge(result_added, (l * 2 + 1) * (NC - 1))
                    sum_tokens(stat_bank["attn"], squares[:, 0, :])

                def token_factors():
                    spread_factors(l, "var")
                    spread_factors(l, "attn")

                def conv_statistic():
                    pe.wait_ge(result_added, (l + 1) * 2 * (NC - 1))
                    statistic("conv", squares[:, 0, :])

                in_tile(0, {7: lambda: x_statistic(l, "mix")})
                for t in range(1, 9):
                    in_tile(t)
                pe.wait_ge(evicted, turn_no(l, MIX_T + IN_TILES.index("v")) + 1 + BANKS)
                pe.wait_ge(std_made, root_no(l, "mix") + 1)
                for b in range(NB):
                    last = nc.tensor.transpose(side_bank[:, b * P:(b + 1) * P],
                                               work[:, IN_TILES.index("v") % BANKS, b * P:(b + 1) * P], ident[:])
                last.then_inc(v_turned, 1)
                for t in range(9, 12):
                    in_tile(t)
                half_tile(12, 0)
                half_tile(12, 1)
                pe.wait_ge(qk_split, l * (NC + 1) + NC + 1)
                ahead = [(g, c) for g in range(AHEAD) for c in range(GROUP)]
                for g, c in ahead[:3]:
                    scores(g, c)
                half_tile(13, 0)
                for g, c in ahead[3:6]:
                    scores(g, c)
                half_tile(13, 1)
                for g, c in ahead[6:]:
                    scores(g, c)
                pe.wait_ge(v_split, l + 1)
                for g in range(N_GROUPS):
                    for c in range(GROUP):
                        turn_weights(g, c)
                        if g + AHEAD < N_GROUPS:
                            scores(g + AHEAD, c)
                        if c == 2 and g:
                            weigh_values(g - 1)
                assert ATT["turned", N_GROUPS - 1, 0] % ATT_BANKS == 0
                pe.wait_ge(att_freed, l * len(ATT) + ATT["turned", N_GROUPS - 1, 0] + 1)
                pe.wait_ge(channels_added, (l + 1) * (NC - 1))
                statistic("mean", channel_sum[:])
                weigh_values(N_GROUPS - 1)

                out_tiles(16, OUT_A_TURN, xs_hi, xs_lo, 0,
                          {(2, 0): token_statistics, (3, 0): token_factors})
                out_tiles(20, OUT_C_TURN, y_hi, y_lo, NC,
                          {(0, 1): conv_statistic})
                ffn_steps(l, FFN_SLOTS + MIX_SLOTS, FFN_TURNS + MIX_TURNS, NF, prep_no(l, 2), "ffn2")
            pe.wait_ge(sq_added, (DEPTH * 3 + 1) * ND)
            sum_tokens(side_bank, sq_sum[:])
            spread_factors(DEPTH, "ffn1")


def by_partition(v):
    return v.reshape(v.shape[0], -1, P).transpose(0, 2, 1)


def tiles_of(w, n_out):
    *lead, k, n = w.shape
    w = w.reshape(*lead, k // P, P, n // n_out, n_out)
    d = len(lead)
    w = w.transpose(*range(d), d + 2, d + 1, d, d + 3)
    return w.reshape(*lead, n // n_out, P, k // P * n_out)


def heads_paired(v, axis):
    shape = v.shape
    v = v.reshape(*shape[:axis], N_KV_HEADS, GROUP, HEAD_DIM, *shape[axis + 1:])
    return v.swapaxes(axis, axis + 1).reshape(shape)


def kernel(**inputs):
    import concourse.bacc as bacc
    from concourse.bass_utils import run_bass_kernel_spmd

    a = {k: np.asarray(v) for k, v in inputs.items()}
    next_norm = np.concatenate([a["ffn1_norm"][1:], a["final_norm"][None]], axis=0)
    conv_w = a["conv_w"].transpose(0, 2, 1).reshape(DEPTH, NC, P, CONV_WIDTH).transpose(0, 2, 1, 3)
    params = np.concatenate([
        by_partition(a["mix_norm"]), by_partition(a["ffn2_norm"]), by_partition(next_norm),
        conv_w.reshape(DEPTH, P, NC * CONV_WIDTH), by_partition(a["conv_b"]), by_partition(a["conv_ln_g"]),
        by_partition(a["conv_ln_b"]), by_partition(a["out_norm_conv"]),
        by_partition(heads_paired(a["out_norm_attn"], 1)),
        np.broadcast_to(a["attn_sink"][:, None, :], (DEPTH, P, N_Q_HEADS)),
    ], axis=2)

    def gate_up(ffn):
        both = np.stack([tiles_of(a[f"{ffn}_w_gate"], P), tiles_of(a[f"{ffn}_w_up"], P)], axis=2)
        return both.reshape(DEPTH, 2 * NF, P, 8 * P)

    w_in = a["w_in"]
    conv_in, q_in, kv_in = w_in[..., :2 * D_CONV], w_in[..., 2 * D_CONV:3 * D_CONV], w_in[..., 3 * D_CONV:]
    in_tiles = tiles_of(np.concatenate([conv_in, heads_paired(q_in, 2), kv_in], axis=2), P)
    order = {"a": 0, "g": NC, "q": 2 * NC, "k": 3 * NC, "v": 3 * NC + 1}
    in_order = [order[t[0]] + int(t[1:] or 0) for t in IN_TILES]
    w_out = a["w_out"]
    out_a = tiles_of(heads_paired(w_out[:, D_CONV:], 1), P)
    out_c = tiles_of(w_out[:, :D_CONV], P)
    pair = [t.reshape(DEPTH, ND // 2, 2, P, 4 * P).transpose(0, 1, 3, 2, 4).reshape(DEPTH, ND // 2, P, 8 * P)
            for t in (out_a, out_c)]
    arrays = {
        "xT": a["x"].reshape(SEQ, D_MODEL).T,
        "first_gain": by_partition(a["ffn1_norm"])[0],
        "params": params,
        "w_gu": np.stack([gate_up("ffn1"), gate_up("ffn2")], axis=1),
        "w_down": np.stack([tiles_of(a["ffn1_w_down"], P), tiles_of(a["ffn2_w_down"], P)], axis=1),
        "w_in": in_tiles[:, in_order],
        "w_out": np.concatenate(pair, axis=1),
    }
    arrays = {k: np.ascontiguousarray(v) for k, v in arrays.items()}
    nc = bacc.Bacc("TRN2", target_bir_lowering=False, num_devices=1)
    args = [nc.dram_tensor(k, v.shape, mybir.dt.from_np(v.dtype), kind="ExternalInput").ap()
            for k, v in arrays.items()]
    out = nc.dram_tensor("out", (D_MODEL, SEQ), F32, kind="ExternalOutput").ap()
    encoder(nc, *args, out)
    r = run_bass_kernel_spmd(nc, [arrays], core_ids=[0])
    return np.ascontiguousarray(r.results[0]["out"].T).reshape(1, SEQ, D_MODEL)
```
